# Optimizing a Trainium2 kernel written in Bass

```python
import jax, jax.numpy as jnp
from jax import lax
import numpy as np

D_MODEL = 1024
BATCH = 1
SEQ = 256
DEPTH = 2

EPS = 1e-6
HEAD_DIM = 64
ROPE_THETA = 10000.0
BLOCK = 128
SWA_HEADS = 8
SWA_KV_HEADS = 2
SWA_WINDOW = BLOCK
DSA_HEADS = 8
DSA_KV_HEADS = 2
IDX_HEADS = 4
IDX_DIM = 64
DSA_TOPK = 256
RET_HEADS = 4
RET_KEY_DIM = 64
RET_VAL_DIM = 128
RET_CHUNK = 128
POOL_WINDOWS = (2, 4, 8, 16)
POOL_GROUP_DIM = 128
N_BRANCH = 4
BRANCH_WIDTH = 512
MEM_LEN = 256
X_HEADS = 4
X_HEAD_DIM = D_MODEL // X_HEADS
D_FF = (7 * D_MODEL) // 2
N_EXPERTS = 8
TOP_K = 2

IN_SIZES = (
    SWA_HEADS * HEAD_DIM, SWA_KV_HEADS * HEAD_DIM, SWA_KV_HEADS * HEAD_DIM,
    DSA_HEADS * HEAD_DIM, DSA_KV_HEADS * HEAD_DIM, DSA_KV_HEADS * HEAD_DIM,
    IDX_HEADS * IDX_DIM, IDX_DIM, IDX_HEADS,
    RET_HEADS * RET_KEY_DIM, RET_HEADS * RET_KEY_DIM, RET_HEADS * RET_VAL_DIM, RET_HEADS * RET_VAL_DIM,
    len(POOL_WINDOWS) * POOL_GROUP_DIM,
    N_BRANCH * D_MODEL,
)
D_IN = sum(IN_SIZES)

kernel_name = "hybrid_gated_parallel_mixer_block"

def rms_norm(x, g):
    xf = x.astype(jnp.float32)
    y = xf * lax.rsqrt(jnp.mean(xf * xf, axis=-1, keepdims=True) + EPS)
    return (y * g.astype(jnp.float32)).astype(x.dtype)

def rope_tables(positions):
    inv = 1.0 / (ROPE_THETA ** (jnp.arange(0, HEAD_DIM, 2, dtype=jnp.float32) / HEAD_DIM))
    ang = positions.astype(jnp.float32)[..., None] * inv
    return jnp.cos(ang)[:, :, None, :], jnp.sin(ang)[:, :, None, :]

def apply_rope(x, cos, sin):
    x1, x2 = jnp.split(x.astype(jnp.float32), 2, axis=-1)
    return jnp.concatenate([x1 * cos - x2 * sin, x2 * cos + x1 * sin], axis=-1).astype(x.dtype)

def sliding_window_attention(q, k, v, sink):
    B, T, Hq, Dh = q.shape
    Hkv = k.shape[2]
    G = Hq // Hkv
    nb = T // BLOCK
    qb = q.reshape(B, nb, BLOCK, Hkv, G, Dh)
    kb = k.reshape(B, nb, BLOCK, Hkv, Dh)
    vb = v.reshape(B, nb, BLOCK, Hkv, Dh)
    prev = lambda z: jnp.concatenate([jnp.zeros_like(z[:, :1]), z[:, :-1]], axis=1)
    kw = jnp.concatenate([prev(kb), kb], axis=2)
    vw = jnp.concatenate([prev(vb), vb], axis=2)
    s = jnp.einsum("bnqhgd,bnkhd->bnhgqk", qb, kw).astype(jnp.float32) * (Dh ** -0.5)
    qi = jnp.arange(BLOCK)[:, None] + BLOCK
    ki = jnp.arange(2 * BLOCK)[None, :]
    rel = qi - ki
    band = (rel >= 0) & (rel < SWA_WINDOW)
    blk = jnp.arange(nb)[:, None, None]
    mask = band[None] & ((blk > 0) | (ki >= BLOCK)[None])
    s = jnp.where(mask[None, :, None, None], s, -jnp.inf)
    sk = sink.astype(jnp.float32).reshape(Hkv, G)[None, None, :, :, None, None]
    m = jnp.maximum(jnp.max(s, axis=-1, keepdims=True), sk)
    p = jnp.exp(s - m)
    p = p / (jnp.sum(p, axis=-1, keepdims=True) + jnp.exp(sk - m))
    o = jnp.einsum("bnhgqk,bnkhd->bnqhgd", p.astype(v.dtype), vw)
    return o.reshape(B, T, Hq * Dh)

def dsa_attention(q, k, v, q_idx, k_idx, w_idx):
    B, T, Hq, Dh = q.shape
    Hkv = k.shape[2]
    G = Hq // Hkv
    nb = T // BLOCK
    n_sel = min(DSA_TOPK, T // 4)
    to_blocks = lambda z: jnp.moveaxis(z.reshape(B, nb, BLOCK, *z.shape[2:]), 1, 0)
    gather = jax.vmap(lambda table, idx: table[idx])
    key_pos = jnp.arange(T)

    def one_block(args):
        q_b, qi_b, wi_b, start = args
        t = start + jnp.arange(BLOCK)
        logits = jnp.einsum("bqhd,bsd->bqhs", qi_b, k_idx).astype(jnp.float32) * (IDX_DIM ** -0.5)
        score = jnp.einsum("bqhs,bqh->bqs", jax.nn.relu(logits), wi_b.astype(jnp.float32))
        causal = key_pos[None, :] <= t[:, None]
        score = jnp.where(causal[None], score, -jnp.inf)
        _, idx = lax.top_k(score, n_sel)
        valid = idx <= t[None, :, None]
        k_sel = gather(k, idx)
        v_sel = gather(v, idx)
        qg = q_b.reshape(B, BLOCK, Hkv, G, Dh)
        s = jnp.einsum("bqhgd,bqkhd->bqhgk", qg, k_sel).astype(jnp.float32) * (Dh ** -0.5)
        s = jnp.where(valid[:, :, None, None, :], s, -jnp.inf)
        p = jax.nn.softmax(s, axis=-1)
        o = jnp.einsum("bqhgk,bqkhd->bqhgd", p.astype(v.dtype), v_sel)
        return o.reshape(B, BLOCK, Hq * Dh)

    starts = jnp.arange(nb, dtype=jnp.int32) * BLOCK
    out = lax.map(one_block, (to_blocks(q), to_blocks(q_idx), to_blocks(w_idx), starts))
    return jnp.moveaxis(out, 0, 1).reshape(B, T, Hq * Dh)

def retention(q, k, v, g):
    B, T, H, Dk = q.shape
    Dv = v.shape[-1]
    C = RET_CHUNK
    nc = T // C
    f32 = jnp.float32
    log_gamma = jnp.log1p(-(2.0 ** (-5.0 - jnp.arange(H, dtype=f32))))
    pos = jnp.arange(C, dtype=f32)
    rel = pos[:, None] - pos[None, :]
    decay = jnp.where(rel >= 0, jnp.exp(log_gamma[:, None, None] * jnp.maximum(rel, 0.0)), 0.0)
    q_decay = jnp.exp(log_gamma[:, None] * (pos + 1.0))[None, :, :, None]
    k_decay = jnp.exp(log_gamma[:, None] * (C - 1.0 - pos))[None, :, :, None]
    chunk_decay = jnp.exp(log_gamma * C)[None, :, None, None]
    to_chunks = lambda z: z.astype(f32).reshape(B, nc, C, H, z.shape[-1]).transpose(1, 0, 3, 2, 4)
    qc, kc, vc = to_chunks(q), to_chunks(k * (Dk ** -0.5)), to_chunks(v)

    def step(state, inp):
        qb, kb, vb = inp
        inner = jnp.einsum("bhnm,bhmv->bhnv", jnp.einsum("bhnd,bhmd->bhnm", qb, kb) * decay, vb)
        cross = jnp.einsum("bhnd,bhdv->bhnv", qb, state) * q_decay
        state = state * chunk_decay + jnp.einsum("bhmd,bhmv->bhdv", kb * k_decay, vb)
        return state, inner + cross

    state0 = jnp.zeros((B, H, Dk, Dv), f32)
    _, out = lax.scan(step, state0, (qc, kc, vc))
    out = out.transpose(1, 0, 3, 2, 4).reshape(B, T, H, Dv)
    out = out * lax.rsqrt(jnp.mean(out * out, axis=-1, keepdims=True) + EPS)
    return (jax.nn.silu(g.astype(f32)) * out.reshape(B, T, H * Dv)).astype(v.dtype)

def multiscale_pool(u, pool_w, pool_scale):
    B, T, _ = u.shape
    G = len(POOL_WINDOWS)
    uf = u.astype(jnp.float32).reshape(B, T, G, POOL_GROUP_DIM)
    csum = jnp.cumsum(uf, axis=1)
    t = jnp.arange(T)
    pooled = []
    for gi, w in enumerate(POOL_WINDOWS):
        c = csum[:, :, gi]
        lag = jnp.pad(c, ((0, 0), (w, 0), (0, 0)))[:, :T]
        cnt = jnp.minimum(t + 1, w).astype(jnp.float32)[None, :, None]
        pooled.append((c - lag) / cnt)
    pooled = jnp.stack(pooled, axis=2)
    y = jnp.einsum("btgc,gcd->btgd", pooled - uf, pool_w.astype(jnp.float32))
    return (y.reshape(B, T, G * POOL_GROUP_DIM) * pool_scale.astype(jnp.float32)).astype(u.dtype)

def token_mixer(h, cos, sin, w_in, sink, w_branch, w_out, pool_w, pool_scale):
    B, T, _ = h.shape
    proj = h @ w_in
    splits = np.cumsum(IN_SIZES)[:-1].tolist()
    (a_q, a_k, a_v, b_q, b_k, b_v, i_q, i_k, i_w,
     r_q, r_k, r_v, r_g, p_u, gates) = jnp.split(proj, splits, axis=-1)
    heads = lambda z, n: z.reshape(B, T, n, -1)
    rope = lambda z: apply_rope(z, cos, sin)
    o_a = sliding_window_attention(rope(heads(a_q, SWA_HEADS)), rope(heads(a_k, SWA_KV_HEADS)),
                                   heads(a_v, SWA_KV_HEADS), sink)
    o_b = dsa_attention(rope(heads(b_q, DSA_HEADS)), rope(heads(b_k, DSA_KV_HEADS)),
                        heads(b_v, DSA_KV_HEADS), rope(heads(i_q, IDX_HEADS)),
                        rope(i_k[:, :, None, :])[:, :, 0], i_w * (IDX_HEADS ** -0.5))
    o_c = retention(rope(heads(r_q, RET_HEADS)), rope(heads(r_k, RET_HEADS)),
                    heads(r_v, RET_HEADS), r_g)
    o_d = multiscale_pool(p_u, pool_w, pool_scale)
    branches = jnp.stack([o_a, o_b, o_c, o_d], axis=2)
    up = jnp.einsum("btnc,ncd->btnd", branches, w_branch)
    gate = jax.nn.sigmoid(gates.reshape(B, T, N_BRANCH, D_MODEL).astype(jnp.float32)).astype(h.dtype)
    merged = jnp.sum(gate * up, axis=2)
    return merged @ w_out

def memory_cross_attention(h, m, w_xq, w_xkv, w_xo):
    B, T, _ = h.shape
    M = m.shape[1]
    q = (h @ w_xq).reshape(B, T, X_HEADS, X_HEAD_DIM)
    k, v = jnp.split(m @ w_xkv, 2, axis=-1)
    k = k.reshape(B, M, X_HEADS, X_HEAD_DIM)
    v = v.reshape(B, M, X_HEADS, X_HEAD_DIM)
    s = jnp.einsum("bthd,bmhd->bhtm", q, k).astype(jnp.float32) * (X_HEAD_DIM ** -0.5)
    p = jax.nn.softmax(s, axis=-1)
    o = jnp.einsum("bhtm,bmhd->bthd", p.astype(v.dtype), v).reshape(B, T, X_HEADS * X_HEAD_DIM)
    return o @ w_xo

def swiglu(h, w_gu, w_down):
    g, u = jnp.split(h @ w_gu, 2, axis=-1)
    return (jax.nn.silu(g) * u) @ w_down

def moe_ffn(h, router_w, w_gu, w_down):
    logits = (h @ router_w).astype(jnp.float32)
    top_val, top_idx = lax.top_k(logits, TOP_K)
    top_w = jax.nn.softmax(top_val, axis=-1)
    gate = jnp.sum(jax.nn.one_hot(top_idx, N_EXPERTS, dtype=jnp.float32) * top_w[..., None], axis=-2)
    gate = gate.astype(h.dtype)
    out = jnp.zeros_like(h)
    for e in range(N_EXPERTS):
        out = out + gate[..., e:e + 1] * swiglu(h, w_gu[e], w_down[e])
    return out

def setup_inputs(seed: int = 0) -> dict:
    key = jax.random.key(seed)
    ks = jax.random.split(key, 24)
    f32 = jnp.float32
    n_dense = (DEPTH + 1) // 2
    n_moe = DEPTH // 2
    n_pool = len(POOL_WINDOWS)
    xw = X_HEADS * X_HEAD_DIM

    def dense(k, shape, fan_in):
        return jax.random.normal(k, shape, f32) * (fan_in ** -0.5)

    def gain(k, shape, scale=0.02):
        return 1.0 + scale * jax.random.normal(k, shape, f32)

    return {
        "x": jax.random.normal(ks[0], (BATCH, SEQ, D_MODEL), f32),
        "mem": jax.random.normal(ks[1], (BATCH, MEM_LEN, D_MODEL), f32),
        "positions": jnp.arange(SEQ, dtype=jnp.int32)[None, :]
        + jax.random.randint(ks[2], (BATCH, 1), 0, 1024, dtype=jnp.int32),
        "norm_mix": gain(ks[3], (DEPTH, D_MODEL)),
        "w_in": dense(ks[4], (DEPTH, D_MODEL, D_IN), D_MODEL),
        "attn_sink": 0.5 * jax.random.normal(ks[5], (DEPTH, SWA_HEADS), f32),
        "w_branch": dense(ks[6], (DEPTH, N_BRANCH, BRANCH_WIDTH, D_MODEL), BRANCH_WIDTH),
        "w_out": dense(ks[7], (DEPTH, D_MODEL, D_MODEL), D_MODEL),
        "pool_w": dense(ks[8], (DEPTH, n_pool, POOL_GROUP_DIM, POOL_GROUP_DIM), POOL_GROUP_DIM),
        "pool_scale": gain(ks[9], (DEPTH, n_pool * POOL_GROUP_DIM), 0.1),
        "norm_cross": gain(ks[10], (DEPTH, D_MODEL)),
        "norm_mem": gain(ks[11], (DEPTH, D_MODEL)),
        "w_xq": dense(ks[12], (DEPTH, D_MODEL, xw), D_MODEL),
        "w_xkv": dense(ks[13], (DEPTH, D_MODEL, 2 * xw), D_MODEL),
        "w_xo": dense(ks[14], (DEPTH, xw, D_MODEL), xw),
        "norm_ffn": gain(ks[15], (DEPTH, D_MODEL)),
        "dense_w_gu": dense(ks[16], (n_dense, D_MODEL, 2 * D_FF), D_MODEL),
        "dense_w_down": dense(ks[17], (n_dense, D_FF, D_MODEL), D_FF),
        "router_w": dense(ks[18], (n_moe, D_MODEL, N_EXPERTS), D_MODEL),
        "moe_w_gu": dense(ks[19], (n_moe, N_EXPERTS, D_MODEL, 2 * D_FF), D_MODEL),
        "moe_w_down": dense(ks[20], (n_moe, N_EXPERTS, D_FF, D_MODEL), D_FF),
        "norm_final": gain(ks[21], (D_MODEL,)),
    }

def reference(x, mem, positions, norm_mix, w_in, attn_sink, w_branch, w_out, pool_w, pool_scale,
              norm_cross, norm_mem, w_xq, w_xkv, w_xo, norm_ffn, dense_w_gu, dense_w_down,
              router_w, moe_w_gu, moe_w_down, norm_final):
    cos, sin = rope_tables(positions)
    for layer in range(DEPTH):
        h = rms_norm(x, norm_mix[layer])
        x = x + token_mixer(h, cos, sin, w_in[layer], attn_sink[layer], w_branch[layer],
                            w_out[layer], pool_w[layer], pool_scale[layer])
        h = rms_norm(x, norm_cross[layer])
        m = rms_norm(mem, norm_mem[layer])
        x = x + memory_cross_attention(h, m, w_xq[layer], w_xkv[layer], w_xo[layer])
        h = rms_norm(x, norm_ffn[layer])
        if layer % 2 == 0:
            x = x + swiglu(h, dense_w_gu[layer // 2], dense_w_down[layer // 2])
        else:
            x = x + moe_ffn(h, router_w[layer // 2], moe_w_gu[layer // 2], moe_w_down[layer // 2])
    return rms_norm(x, norm_final)


_drawn_inputs = setup_inputs


def setup_inputs(seed=0):
    import zlib

    import numpy as np

    out = dict(_drawn_inputs(seed))
    spreads = {}
    factors = {'attn_sink': 4.372, 'norm_cross': 2.667, 'norm_final': 2.747}
    for name, (base, spread) in spreads.items():
        noise = np.random.default_rng([zlib.crc32(name.encode()), seed]).standard_normal(out[name].shape)
        drawn = base * np.exp(spread * noise) if base else spread * noise
        out[name] = __import__('jax').numpy.asarray(drawn.astype(out[name].dtype))
    for name, factor in factors.items():
        out[name] = (out[name] * factor).astype(out[name].dtype)
    return out
```

```python
import math
from contextlib import ExitStack

import numpy as np

import concourse.bass as bass
from concourse import mybir

F32 = mybir.dt.float32
F32R = mybir.dt.float32r
I32 = mybir.dt.int32
U32 = mybir.dt.uint32
ALU = mybir.AluOpType
ACT = mybir.ActivationFunctionType
AX = mybir.AxisListType

P = 128
EPS = 1e-6
ROPE_THETA = 10000.0
HEAD_DIM = 64
N_SEL = 64
NEG = -1.0e30
TAKEN = -3.0e38
TWO_PI = 2.0 * math.pi
PI2_A = 6.28125
PI2_B = 4059 / 2.0 ** 21
PI2_C = TWO_PI - PI2_A - PI2_B
TRIG_DECAY = 4
TRIG_SINES = 8
TRIG_REDUCED = 19
ROUTE_DIFF = 6
ROUTE_MEMBER = 19
NO_SLOT = 1000.0
RAW_SLOTS = 3
CYCLE = 6
SPLIT_SLOTS = 3
UNIT = 512


class Chunk:

    def __init__(self, name, first_block, ktiles, n, parity):
        self.name, self.first_block, self.ktiles, self.n, self.parity = name, first_block, ktiles, n, parity
        self.blocks = ktiles // 4
        self.last_block = first_block + self.blocks - 1


def plan_chunks():
    spec = [("pu", 8, 512), ("idx", 8, 324), ("bq", 8, 512), ("kv", 8, 512), ("aq", 8, 512),
            ("rqk", 8, 512), ("rv", 8, 512), ("rg", 8, 512)]
    for branch in "DCAB":
        for half in range(2):
            spec += [(f"gate{branch}{half}", 8, 512), (f"up{branch}{half}", 4, 512)]
    spec += [(f"out{h}", 8, 512) for h in range(2)]
    spec += [(name, 8, 512) for name in ("xkv0", "xkv1", "xq0", "xq1", "xkv2", "xkv3")]
    spec += [(f"xo{c}", 8, 512) for c in range(2)]
    chunks, b = [], 0
    for i, (name, kt, n) in enumerate(spec):
        chunks.append(Chunk(name, b, kt, n, i % 2))
        b += kt // 4
    return chunks, b


class Signal:

    def __init__(self, sem, steps):
        self.sem, self.steps = sem, list(steps)

    def at(self, turn, step):
        return turn * len(self.steps) + (self.steps.index(step) + 1)


GROUPS = ["a0", "a1", "b0", "b1"]


def small_uses():
    return (["h0", "h1", "h2", "h3", "pool0", "pool1", "pooly0", "pooly1", "tr_idx0", "tr_idx1",
             "tr_bq0", "tr_bq1", "lg0a", "lg0b", "tr_kv0", "tr_kv1", "lg1a", "lg1b", "tr_aq0", "tr_aq1",
             "tr_rqk0", "tr_rqk1", "s_a0_0", "s_a0_1", "st0", "st1", "st2", "st3", "ro0", "ro1",
             "p_a0_0", "p_a0_1", "o_a0", "tC0", "tC1", "s_a1_0", "s_a1_1", "s_a1_2", "s_a1_3",
             "p_a1_0", "p_a1_1", "p_a1_2", "p_a1_3", "o_a1", "s_b0_0", "s_b0_1", "tA0", "tA1",
             "p_b0_0", "p_b0_1", "o_b0", "s_b1_0", "s_b1_1", "s_b1_2", "s_b1_3",
             "p_b1_0", "p_b1_1", "p_b1_2", "p_b1_3", "o_b1", "tB0", "tB1",
             "m0", "m1", "m2", "m3", "c0", "c1", "c2", "c3"]
            + [f"xk{i}" for i in range(4)] + [f"xq{i}" for i in range(4)]
            + [f"{use}{i}" for use in ("xs0", "xp0", "xs1", "xo0", "xp1", "xo1") for i in range(2)]
            + [f"xt{i}" for i in range(4)] + [f"f{i}" for i in range(4)])


def build(nc, x_in, mem_in, positions, norm_mix, w_in, attn_sink, w_branch, w_out, pool_w, pool_scale,
          norm_cross, norm_mem, w_xq, w_xkv, w_xo, norm_ffn, dense_w_gu, dense_w_down, router_w,
          moe_w_gu, moe_w_down, norm_final, out):
    DEPTH, D = norm_mix.shape
    T = x_in.shape[1]
    NT = T // P
    KD = D // P
    E, F = moe_w_down.shape[1], moe_w_down.shape[2]
    UNITS = F // UNIT
    JOBS_MAX = E + 3
    assert NT == 2 and KD == 8 and UNITS == 7 and E == 8 and DEPTH == 2

    CHUNKS, MIX_BLOCKS = plan_chunks()
    CH = {c.name: c for c in CHUNKS}
    UNIT_BLOCKS = 6
    FFN_BLOCKS = UNITS * UNIT_BLOCKS
    LAYER_BLOCKS = MIX_BLOCKS + FFN_BLOCKS
    assert MIX_BLOCKS % CYCLE == 0 and FFN_BLOCKS % CYCLE == 0 and CYCLE == 2 * RAW_SLOTS == 2 * SPLIT_SLOTS
    SMALL = small_uses()
    small_bank = {name: i % 4 for i, name in enumerate(SMALL)}
    small_turn = {name: i // 4 for i, name in enumerate(SMALL)}
    per_bank = [sum(1 for i in range(len(SMALL)) if i % 4 == b) for b in range(4)]

    ctx = ExitStack()
    with ctx:
        def sb(name, shape, dt=F32):
            return ctx.enter_context(nc.sbuf_tensor(name, shape, dt))

        def sem(name):
            return ctx.enter_context(nc.semaphore(name))

        x = sb("x", [P, NT, D])
        tok = sb("tok", [P, NT, D])
        memT = sb("memT", [P, KD, T])
        stat0 = sb("stat0", [P, 2, 8, T], F32R)
        stat1 = sb("stat1", [P, 2, 8, T], F32R)
        raw = sb("raw", [P, RAW_SLOTS, 4, UNIT])
        w_hi = sb("w_hi", [P, SPLIT_SLOTS, 4, UNIT], F32R)
        w_lo = sb("w_lo", [P, SPLIT_SLOTS, 4, UNIT], F32R)
        rvg = sb("rvg", [P, 2, NT, 512])
        pu_rv = rvg[:, 0, :, :]
        rg = rvg[:, 1, :, :]
        v_ab = sb("v_ab", [P, NT, 2, 128])
        o_buf = sb("o_buf", [P, 2, NT, 512])
        heads_t = sb("heads_t", [P, 17, T])
        area_a = sb("area_a", [P, 2048])
        area_b = sb("area_b", [P, 2048])
        roped = sb("roped", [P, NT, 512])
        gate = sb("gate", [P, NT, 512])
        work = sb("work", [P, T])
        sel_mask = sb("sel_mask", [P, NT, T])
        ident = sb("ident", [P, P])
        decay = sb("decay", [P, 4, T])
        pool_m0 = sb("pool_m0", [P, 4, 144])
        pool_m1 = sb("pool_m1", [P, 4, P])
        mask_a = sb("mask_a", [P, T])
        mask_c = sb("mask_c", [P, T])
        cos2 = sb("cos2", [P, NT, 64])
        sin1 = sb("sin1", [P, NT, 32])
        nsin1 = sb("nsin1", [P, NT, 32])
        gains = sb("gains", [P, 72])
        pw = sb("pw", [P, 4, P])
        sink_sb = sb("sink_sb", [P, DEPTH, 8])
        rw = sb("rw", [P, KD, 8])
        rw_hi = sb("rw_hi", [P, KD, 8], F32R)
        rw_lo = sb("rw_lo", [P, KD, 8], F32R)
        zeros = sb("zeros", [P, P], F32R)
        gn = sb("gn", [P, 36])
        sink_now = sb("sink_now", [P, 8])
        pos_i = sb("pos_i", [P, NT], I32)
        pos_f = sb("pos_f", [P, NT])
        eps_sb = sb("eps_sb", [P, 1])
        slots_iota = sb("slots_iota", [P, P])
        lane8 = sb("lane8", [P, 8])
        triu = sb("triu", [P, P])
        ones = sb("ones", [P, P])
        ss = sb("ss", [P, NT])
        rt = sb("rt", [P, NT])
        rs = sb("rs", [P, NT])
        iw = sb("iw", [P, NT, 4])
        smx = sb("smx", [P, 8])
        sm = sb("sm", [P, 8])
        snm = sb("snm", [P, 8])
        sds = sb("sds", [P, 8])
        ses = sb("ses", [P, 8])
        ssum = sb("ssum", [P, 8])
        sinv = sb("sinv", [P, 8])
        top8 = sb("top8", [P, 8])
        rss = sb("rss", [P, NT, 4])
        rrt = sb("rrt", [P, NT, 4])
        rrs = sb("rrs", [P, NT, 4])

        def view(area, lo, *shape):
            n = int(np.prod(shape))
            names = "abcd"[:len(shape)]
            pat = f"p ({' '.join(names)}) -> p {' '.join(names)}"
            return area[:, lo:lo + n].rearrange(pat, **dict(zip(names, shape)))

        scores = view(area_a, 0, 8, T)
        rope1 = view(area_a, 0, NT, 512)
        rope2 = view(area_a, 1024, NT, 512)
        probs_t = view(area_b, 0, 16, P)
        pooled_t = view(area_b, 0, 4, T)
        relu_sb = view(area_b, 1024, 4, T)
        xs_scores = view(area_a, 0, 4, T)
        q_tok = view(area_b, 0, NT, D)
        k_tok = view(area_a, 0, NT, D)
        v_tok = o_buf[:, :, :, :].rearrange("p a t n -> p (a t n)").rearrange("p (t n) -> p t n", t=NT)
        decayed = tok[:, :, :].rearrange("p t d -> p (t d)")[:, 0:1536].rearrange("p (h n) -> p h n", h=4)
        x_probs_t = view(area_b, 0, 8, P)
        kT_x = heads_t[:, 0:8, :]
        qT_x = heads_t[:, 8:16, :]
        merged = tok
        hid = view(area_a, 0, NT, 512)
        silu_g = view(area_b, 0, NT, 512)
        flat_heads = heads_t[:, :, :].rearrange("p a t -> p (a t)")
        y_sb = view(flat_heads, 2048, D)
        pick = view(flat_heads, 3072, NT, P)
        wpick = view(flat_heads, 3328, NT, P)
        wpick_t = view(flat_heads, 3584, NT, P)
        rt_area = view(flat_heads, 3840, 512)
        final_gain = gate[:, :, :].rearrange("p t n -> p (t n)")
        rt_diff, rt_exp = rt_area[:, 132:134], rt_area[:, 134:136]
        expert_raw = ([raw[:, i, :, :] for i in range(RAW_SLOTS)]
                      + [memT[:, :, :].rearrange("p (k a) t -> p k (a t)", k=4),
                         o_buf[:, :, :, :].rearrange("p a t n -> p (a t) n"),
                         rvg[:, :, :, :].rearrange("p a t n -> p (a t) n")])
        EXPERT_SLOTS = len(expert_raw)
        slot_of = sb("slot_of", [P, NT, JOBS_MAX + 1])
        gate_of = sb("gate_of", [P, NT, JOBS_MAX + 1])
        route_i = sb("route_i", [P, 4], I32)

        gain_rows = area_b[0:72, 1024:1024 + P]
        ang = view(area_b, 0, NT, 32)
        turns_f = view(area_b, 64, NT, 32)
        turns_i = area_b[:, 128:192].bitcast(I32).rearrange("p (a b) -> p a b", a=NT)
        red = view(area_b, 192, NT, 32)
        red2 = view(area_b, 256, NT, 32)
        over = view(area_b, 320, NT, 32)
        inv_freq = view(area_b, 384, 32)

        bank = [ctx.enter_context(nc.psum_tensor(f"bank{i}", [P, 512], F32)) for i in range(8)]

        def acc(c, t):
            return bank[2 * c.parity + t]

        def small(name):
            return bank[4 + small_bank[name]]

        inputs_landed = sem("inputs_landed")
        pool_w_landed = sem("pool_w_landed")
        final_landed = sem("final_landed")
        stored = sem("stored")
        raw_landed = [sem(f"raw_landed{i}") for i in range(RAW_SLOTS)]
        expert_landed = [sem(f"expert_landed{i}") for i in range(EXPERT_SLOTS)]
        kv_landed = [sem(f"kv_landed{i}") for i in range(2)]
        hi_done = sem("hi_done")
        lo_done = sem("lo_done")
        block_used = sem("block_used")
        small_full = Signal(sem("small_full"), SMALL)
        bank_free = [Signal(sem(f"bank_free{b}"), [s for s in SMALL if small_bank[s] == b]) for b in range(4)]
        acc_free = [Signal(sem(f"acc_free{q}"), [c.name for c in CHUNKS if c.parity == q and c.name not in ("bq", "aq", "rqk")]) for q in range(2)]

        consts_ready = sem("consts_ready")
        const_step = sem("const_step")
        trig_step = sem("trig_step")
        trig_dve = sem("trig_dve")
        setup_full = sem("setup_full")
        setup_free = sem("setup_free")
        layer_consts = Signal(sem("layer_consts"), ["gains", "scales", "sinks"])
        setup_split = sem("setup_split")

        norm_names = ["mix", "cross", "ffn"]
        norm_act = Signal(sem("norm_act"), [f"{n} {s}" for n in norm_names for s in ("sq", "root", "scaled")])
        norm_dve = Signal(sem("norm_dve"), [f"{n} {s}" for n in norm_names for s in ("sq", "inv", "scaled")])
        ends_act = Signal(sem("ends_act"), ["sq", "root", "scaled"])
        ends_dve = Signal(sem("ends_dve"), ["sq", "inv", "scaled"])
        final_rows = sem("final_rows")
        act_hi = Signal(sem("act_hi"), [f"h{i}" for i in range(4)] + ["pooly0", "pooly1", "tC0", "tC1", "tA0", "tA1",
                                        "tB0", "tB1", "m0", "m1", "m2", "m3", "mem"]
                        + [f"c{i}" for i in range(4)] + [f"xt{i}" for i in range(4)] + [f"f{i}" for i in range(4)])
        mem_split = Signal(sem("mem_split"), ["split"])
        ROPE_CHUNKS = ["idx", "bq", "kv", "aq", "rqk"]
        rope_mult = Signal(sem("rope_mult"), [f"{c}{t}" for c in ROPE_CHUNKS for t in range(NT)])
        rope_add = Signal(sem("rope_add"), [f"{c}{t}" for c in ROPE_CHUNKS for t in range(NT)])
        index_w = Signal(sem("index_w"), ["scaled"])
        weigh = Signal(sem("weigh"), [f"{t} head{h}" for t in range(NT) for h in range(4)])
        rank = Signal(sem("rank"), [f"{t} {s}" for t in range(NT) for s in
                                    ["causal"] + [f"{w}{i}" for i in range(8) for w in ("top", "take")] + ["left", "mask"]])
        rank_alone = sem("rank_alone")
        wait_alone = sem("wait_alone")
        soft_dve = {g: Signal(sem(f"soft_dve_{g}"), ["max", "sunk", "shift", "sink shift", "total", "inv"]
                              if g[0] == "a" else ["max", "shift", "inv"]) for g in GROUPS}
        soft_act = {g: Signal(sem(f"soft_act_{g}"), ["exp"] + (["sink exp"] if g[0] == "a" else [])) for g in GROUPS}
        ret_act = Signal(sem("ret_act"), ["squares", "root"])
        ret_dve = Signal(sem("ret_dve"), ["inv"])
        up_added = Signal(sem("up_added"), [f"{b}{h}" for b in "CAB" for h in range(2)])
        xsoft_dve = Signal(sem("xsoft_dve"), [f"{s}{t}" for t in range(NT) for s in ("max", "shift", "inv")])

        ffn_tr = [Signal(sem(f"ffn_tr{i}"), ["tr"]) for i in range(2)]
        ffn_silu = [Signal(sem(f"ffn_silu{i}"), ["silu"]) for i in range(2)]
        ffn_hid = [Signal(sem(f"ffn_hid{i}"), ["hid"]) for i in range(2)]
        ffn_hi = [Signal(sem(f"ffn_hi{i}"), ["hi"]) for i in range(2)]
        ffn_lo = [Signal(sem(f"ffn_lo{i}"), ["lo"]) for i in range(2)]
        ffn_acc = Signal(sem("ffn_acc"), ["half0", "half1"])
        y_copied = Signal(sem("y_copied"), ["y"])
        pick_ready = Signal(sem("pick_ready"), ["pick", "weighted"])
        gather_full = Signal(sem("gather_full"), ["low", "high"])
        gather_hi = Signal(sem("gather_hi"), ["low", "high"])
        gather_lo = Signal(sem("gather_lo"), ["low", "high"])
        picks_full = Signal(sem("picks_full"), ["picks"])
        picks_copied = Signal(sem("picks_copied"), ["picks"])
        scatter_full = Signal(sem("scatter_full"), ["t0", "t1"])
        scatter_added = Signal(sem("scatter_added"), ["t0", "t1"])
        route_full = sem("route_full")
        route_dve = sem("route_dve")
        route_act = sem("route_act")
        x_stands = sem("x_stands")
        routed = sem("routed")

        N_SMALL_LOADS = 10
        LAYER_6, MIX_6, FFN_6 = LAYER_BLOCKS // CYCLE, MIX_BLOCKS // CYCLE, FFN_BLOCKS // CYCLE

        def number(b):
            return b[0] * CYCLE + b[1]

        def slot(b):
            return b[1] % RAW_SLOTS

        def landed_at(b):
            return (b[0] * 2 + (b[1] // RAW_SLOTS + 1)) * 16

        def expert_slot(b):
            return b[1] % EXPERT_SLOTS

        def expert_landed_at(b):
            return (b[0] + (b[1] // EXPERT_SLOTS + 1 - EXPERTS_BASE)) * 16

        def plus(b, k):
            return (b[0], b[1] + k)

        def chunk_block(layer, c, i):
            return (layer * LAYER_6, c.first_block + i)

        def gu_block(base, u):
            return (base, 0) if isinstance(u, int) and u == 0 else (base + (u - 1), 4)

        def down_block(base, u):
            return (base, FFN_BLOCKS - 2) if isinstance(u, int) and u == UNITS - 1 else (base + (u + 1), 2)

        DENSE_BASE = MIX_6
        EXPERTS_BASE = LAYER_6 + MIX_6

        def job_base(j):
            return j * FFN_6 + EXPERTS_BASE

        def chunk_source(name, i, layer):
            rows = slice(i * 512, (i + 1) * 512)
            w1 = lambda a, lo, n: a[bass.ds(layer, 1), rows, lo:lo + n].rearrange("a (k p) n -> p (a k) n", p=P)
            if name == "kv":
                return w1(w_in, 512, 256)
            if name == "kv second":
                return w1(w_in, 1280, 256)
            if name == "pu":
                return w1(w_in, 3396, 512)
            if name == "idx":
                return w1(w_in, 1536, 324)
            if name == "bq":
                return w1(w_in, 768, 512)
            if name == "aq":
                return w1(w_in, 0, 512)
            if name == "rqk":
                return w1(w_in, 1860, 512)
            if name == "rv":
                return w1(w_in, 2372, 512)
            if name == "rg":
                return w1(w_in, 2884, 512)
            if name.startswith("gate"):
                branch, half = "ABCD".index(name[4]), int(name[5])
                return w1(w_in, 3908 + branch * 1024 + half * 512, 512)
            if name.startswith("up"):
                branch, half = "ABCD".index(name[2]), int(name[3])
                return w_branch[bass.ds(layer, 1), branch, :, half * 512:(half + 1) * 512].rearrange(
                    "a (k p) n -> p (a k) n", p=P)
            lo = int(name[-1]) * 512
            return w1({"out": w_out, "xkv": w_xkv, "xq": w_xq, "xo": w_xo}[name[:-1]], lo, 512)

        def gu_source(w, e, unit, which, i):
            col = unit * UNIT + which * F
            return w[bass.ds(e, 1), i * 512:(i + 1) * 512, bass.ds(col, UNIT)].rearrange(
                "a (k p) n -> p (a k) n", p=P)

        def down_source(w, e, unit, half):
            return w[bass.ds(e, 1), bass.ds(unit * UNIT, UNIT), half * 512:(half + 1) * 512].rearrange(
                "a (k p) n -> p (a k) n", p=P)

        block = ctx.enter_context(nc.Block())

        def bank_sem(name):
            return bank_free[small_bank[name]].sem

        def emptied_at(layer, name):
            return bank_free[small_bank[name]].at(layer, name)

        def acc_signal(c):
            return rope_mult if c.name in ("bq", "aq", "rqk") else acc_free[c.parity]

        def acc_sem(c):
            return acc_signal(c).sem

        def released_at(layer, c):
            return acc_signal(c).at(layer, f"{c.name}1" if c.name in ("bq", "aq", "rqk") else c.name)

        def used_at(b):
            return number(b) + (1 + SPLIT_SLOTS)

        def chunk_at(layer, name):
            return used_at((layer * LAYER_6, CH[name].last_block))

        def heads(ap, n):
            return ap.rearrange("p (h d) -> p h d", h=n)

        def f32_of(ap):
            return ap.bitcast(F32)

        @block.sync
        def _(sp):
            def start(dst, src, landed=inputs_landed):
                sp.dma_start(dst, src).then_inc(landed, 16)

            start(tok[:, :, :], mem_in[0].rearrange("(t p) d -> p t d", p=P))
            start(gain_rows[0:16, :], norm_mix.rearrange("l (k p) -> (l k) p", p=P))
            start(gain_rows[16:32, :], norm_cross.rearrange("l (k p) -> (l k) p", p=P))
            start(gain_rows[32:48, :], norm_mem.rearrange("l (k p) -> (l k) p", p=P))
            start(gain_rows[48:64, :], norm_ffn.rearrange("l (k p) -> (l k) p", p=P))
            start(gain_rows[64:72, :], pool_scale.rearrange("l (k p) -> (l k) p", p=P))
            start(x[:, :, :], x_in[0].rearrange("(t p) d -> p t d", p=P))
            sp.dma_start(pos_i[:, :], positions[0].rearrange("(t p) -> p t", p=P),
                         allow_slow_non_contiguous=True).then_inc(inputs_landed, 16)
            start(rw[:, :, :], router_w[0].rearrange("(k p) e -> p k e", p=P))
            start(sink_sb[:, :, :], attn_sink.rearrange("(a l) h -> a l h", a=1).broadcast_to([P, DEPTH, 8]))
            start(pw[:, :, :], pool_w[0].rearrange("g c d -> c g d"), pool_w_landed)

            def load_block(b, src, width=UNIT, alone=False):
                sp.wait_ge(lo_done, number(b) + 1)
                if alone:
                    sp.sem_inc(wait_alone, 1)
                sp.dma_start(raw[:, slot(b), :, 0:width], src).then_inc(raw_landed[slot(b)], 16)

            def load_first_expert_block(b, src):
                if expert_slot(b) < RAW_SLOTS:
                    sp.wait_ge(lo_done, number(b) + 1)
                else:
                    sp.wait_ge(small_full.sem, small_full.at(1, "xo11"))
                sp.dma_start(expert_raw[expert_slot(b)], src).then_inc(expert_landed[expert_slot(b)], 16)

            def load_expert_block(b, src):
                sp.wait_ge(lo_done, number(b) + (1 + RAW_SLOTS - EXPERT_SLOTS))
                sp.dma_start(expert_raw[expert_slot(b)], src).then_inc(expert_landed[expert_slot(b)], 16)

            def load_gu(w, e, u, base, load):
                for j in range(4):
                    load(plus(gu_block(base, u), j), gu_source(w, e, u, j // 2, j % 2))

            def load_down(w, e, u, base, load):
                for j in range(2):
                    load(plus(down_block(base, u), j), down_source(w, e, u, j))

            def load_ffn(w_gu, w_down, e, base, load):
                load_gu(w_gu, e, 0, base, load)
                with sp.Fori(1, UNITS) as u:
                    load_gu(w_gu, e, u, base, load)
                    load_down(w_down, e, u - 1, base, load)
                load_down(w_down, e, UNITS - 1, base, load)

            with sp.Fori(0, DEPTH) as layer:
                for c in CHUNKS:
                    for i in range(c.blocks):
                        b = chunk_block(layer, c, i)
                        if c.name == "kv":
                            load_block(b, chunk_source("kv", i, layer), 256)
                            sp.dma_start(raw[:, slot(b), :, 256:512], chunk_source("kv second", i, layer)).then_inc(kv_landed[i], 16)
                        else:
                            load_block(b, chunk_source(c.name, i, layer), c.n, c.name in ("aq", "upA0") and i == 0)
                with sp.If(layer == 0):
                    load_ffn(dense_w_gu, dense_w_down, 0, DENSE_BASE, load_block)
                    start(pw[:, :, :], pool_w[1].rearrange("g c d -> c g d"), pool_w_landed)
                with sp.Else():
                    load_gu(moe_w_gu[0], 0, 0, job_base(0), load_first_expert_block)
                    for j in range(4):
                        b = plus(gu_block(job_base(0), 1), j)
                        (load_first_expert_block if j < 2 else load_expert_block)(b, gu_source(moe_w_gu[0], 0, 1, j // 2, j % 2))
                    load_down(moe_w_down[0], 0, 0, job_base(0), load_expert_block)
                    with sp.Fori(2, UNITS) as u:
                        load_gu(moe_w_gu[0], 0, u, job_base(0), load_expert_block)
                        load_down(moe_w_down[0], 0, u - 1, job_base(0), load_expert_block)
                    load_down(moe_w_down[0], 0, UNITS - 1, job_base(0), load_expert_block)
                    with sp.Fori(1, E) as e:
                        load_ffn(moe_w_gu[0], moe_w_down[0], e, job_base(e), load_expert_block)
                sp.nop()
            sp.wait_ge(routed, 1)
            n_more = sp.value_load(route_i[0:1, 3:4], min_val=0, max_val=3)
            with sp.If(n_more > 0):
                with sp.Fori(0, n_more) as k:
                    e = sp.value_load(route_i[0:1, bass.ds(k, 1)], min_val=0, max_val=E - 1)
                    load_ffn(moe_w_gu[0], moe_w_down[0], e, job_base(k + E), load_expert_block)
            sp.nop()
            sp.dma_start(final_gain, norm_final.rearrange("(a d) -> a d", a=1).broadcast_to([P, D])).then_inc(final_landed, 16)
            for t in range(NT):
                sp.wait_ge(final_rows, t + 1)
                sp.dma_start(out[0, t * P:(t + 1) * P, :], tok[:, t, :]).then_inc(stored, 16)
            sp.wait_ge(stored, 16 * NT)

        @block.gpsimd
        def _(gp):
            made = [0]

            def step(ins):
                made[0] += 1
                ins.then_inc(const_step, 1)

            def settle():
                gp.wait_ge(const_step, made[0])

            step(gp.memset(ident[:, :], 0.0))
            for j in range(32):
                inv = np.float32(1.0) / np.float32(ROPE_THETA) ** (np.float32(2 * j) / np.float32(HEAD_DIM))
                step(gp.memset(inv_freq[:, j:j + 1], float(inv)))
            step(gp.memset(eps_sb[:, :], EPS))
            step(gp.memset(ones[:, :], 1.0))
            step(gp.memset(f32_of(zeros[:, :]), 0.0))
            step(gp.iota(work[:, :].bitcast(I32), pattern=[[1, T]], base=0, channel_multiplier=-1))
            settle()
            step(gp.affine_select(out=ident[:, :], in_=ident[:, :], compare_op=ALU.not_equal, fill=1.0, base=0,
                                  pattern=[[-1, P]], channel_multiplier=1))
            settle()
            gp.affine_select(out=triu[:, :], in_=ones[:, :], compare_op=ALU.is_gt, fill=0.0, base=0,
                             pattern=[[1, P]], channel_multiplier=-1).then_inc(consts_ready, 1)
            for g in range(4):
                w = 2 ** (g + 1)
                step(gp.memset(pool_m0[:, g, :], 1.0 / w))
                step(gp.memset(pool_m1[:, g, :], 1.0 / w))
            settle()
            for g in range(4):
                for t in range(2 ** (g + 1) - 1):
                    step(gp.memset(pool_m0[:, g, t:t + 1], 1.0 / (t + 1)))
            settle()
            for g in range(4):
                for m, n in ((pool_m0, 144), (pool_m1, P)):
                    step(gp.affine_select(out=m[:, g, :], in_=m[:, g, :], compare_op=ALU.is_ge, fill=0.0, base=0,
                                          pattern=[[1, n]], channel_multiplier=-1))
            settle()
            for g in range(4):
                for m, n in ((pool_m0, 144), (pool_m1, P)):
                    step(gp.affine_select(out=m[:, g, :], in_=m[:, g, :], compare_op=ALU.is_ge, fill=0.0,
                                          base=2 ** (g + 1) - 1, pattern=[[-1, n]], channel_multiplier=1))
            settle()
            for g in range(4):
                for m in (pool_m0, pool_m1):
                    step(gp.tensor_tensor(m[:, g, 0:P], m[:, g, 0:P], ident[:, :], ALU.subtract))
            step(gp.memset(mask_c[:, :], 0.0))
            settle()
            step(gp.affine_select(out=mask_c[:, :], in_=mask_c[:, :], compare_op=ALU.is_ge, fill=NEG, base=P,
                                  pattern=[[-1, T]], channel_multiplier=1))
            settle()
            gp.affine_select(out=mask_a[:, :], in_=mask_c[:, :], compare_op=ALU.is_ge, fill=NEG, base=-1,
                             pattern=[[1, T]], channel_multiplier=-1).then_inc(consts_ready, 1)
            step(gp.iota(slots_iota[:, :].bitcast(I32), pattern=[[1, P]], base=0, channel_multiplier=0))
            settle()
            step(gp.tensor_copy(slots_iota[:, :], slots_iota[:, :].bitcast(I32)))
            gp.wait_ge(trig_step, TRIG_DECAY)
            settle()
            for h in range(4):
                step(gp.affine_select(out=decay[:, h, :], in_=decay[:, h, :], compare_op=ALU.is_ge, fill=0.0, base=0,
                                      pattern=[[1, T]], channel_multiplier=-1))
            settle()
            gp.tensor_scalar(decay[:, :, :], decay[:, :, :], 0.125, None, ALU.mult).then_inc(consts_ready, 1)

            def added(layer, name, t, out, a, b):
                gp.tensor_tensor(out, a, b, ALU.add).then_inc(rope_add.sem, 1)

            with gp.Fori(0, DEPTH) as layer:
                for n, name in enumerate(ROPE_CHUNKS):
                    for t in range(NT):
                        gp.wait_ge(rope_mult.sem, rope_mult.at(layer, f"{name}{t}"))
                        if n:
                            gp.wait_ge(small_full.sem, small_full.at(layer, f"tr_{ROPE_CHUNKS[n - 1]}{t}"))
                        a, b, o = rope1[:, t, :], rope2[:, t, :], roped[:, t, :]
                        if name == "idx":
                            gp.tensor_tensor(o[:, 0:320], a[:, 0:320], b[:, 0:320], ALU.add)
                            added(layer, name, t, o[:, 320:384], a[:, 256:320], b[:, 256:320])
                        elif name == "kv":
                            added(layer, name, t, o[:, 0:256], a[:, 0:256], b[:, 0:256])
                        elif name in ("bq", "aq"):
                            v = lambda y: y.rearrange("p (g m d) -> p g m d", g=2, m=4)
                            added(layer, name, t, o.rearrange("p (m g d) -> p g m d", g=2, m=4), v(a), v(b))
                        else:
                            added(layer, name, t, o, a, b)

        @block.scalar
        def _(act):
            def hi(b, width=UNIT):
                act.wait_ge(raw_landed[slot(b)], landed_at(b))
                act.wait_ge(block_used, number(b) + 1)
                act.activation(w_hi[:, slot(b), :, 0:width], raw[:, slot(b), :, 0:width], ACT.Copy).then_inc(hi_done, 1)

            def expert_hi(b):
                act.wait_ge(expert_landed[expert_slot(b)], expert_landed_at(b))
                act.wait_ge(block_used, number(b) + 1)
                act.activation(w_hi[:, slot(b), :, :], expert_raw[expert_slot(b)], ACT.Copy).then_inc(hi_done, 1)

            def hi_chunk(layer, c):
                for i in range(c.blocks):
                    if c.name == "kv":
                        act.wait_ge(kv_landed[i], (layer + 1) * 16)
                    hi(chunk_block(layer, c, i), c.n)

            def norm(turn, sig, dve_sig, pre, src, dst):
                act.activation(dst[:, 0, :], src[:, 0, :], ACT.Square, accum_out=ss[:, 0:1]).then_inc(sig.sem, 1)
                act.wait_ge(sig.sem, sig.at(turn, f"{pre}sq"))
                act.wait_ge(dve_sig.sem, dve_sig.at(turn, f"{pre}sq"))
                act.activation(rt[:, :], ss[:, :], ACT.Sqrt, bias=eps_sb[:, 0:1], scale=1.0 / D).then_inc(sig.sem, 1)
                act.wait_ge(dve_sig.sem, dve_sig.at(turn, f"{pre}inv"))
                act.activation(dst[:, 0, :], src[:, 0, :], ACT.Copy, scale=rs[:, 0:1]).then_inc(sig.sem, 1)

            act.wait_ge(inputs_landed, 16 * N_SMALL_LOADS)
            act.wait_ge(consts_ready, 1)
            norm(0, ends_act, ends_dve, "", tok, k_tok)
            act.activation(rw_hi[:, :, :], rw[:, :, :], ACT.Copy).then_inc(setup_split, 1)
            for h in range(4):
                lg = float(np.log1p(-np.float32(2.0 ** (-5.0 - h))))
                act.activation(decay[:, h, :], work[:, :].bitcast(I32), ACT.Exp, scale=lg).then_inc(trig_step, 1)
            act.wait_ge(trig_dve, TRIG_REDUCED)
            act.activation(sin1[:, :, :], red, ACT.Sin).then_inc(trig_step, 1)
            act.activation(nsin1[:, :, :], red, ACT.Sin, scale=-1.0).then_inc(trig_step, 1)
            act.activation(cos2[:, :, 0:32], red2, ACT.Sin).then_inc(trig_step, 1)
            act.activation(cos2[:, :, 32:64], red2, ACT.Sin).then_inc(trig_step, 1)

            def split_scaled(layer, name, dst, pairs):
                act.wait_ge(small_full.sem, small_full.at(layer, name))
                for i, (k, col) in enumerate(pairs):
                    ins = act.activation(dst[:, 0, k, :], small(name)[:, i * T:(i + 1) * T], ACT.Copy, scale=gn[:, col:col + 1])
                ins.then_inc(act_hi.sem, 1)

            def split_rows(layer, name, dst, t):
                act.wait_ge(small_full.sem, small_full.at(layer, name))
                act.activation(dst[:, :, t * P:(t + 1) * P],
                                         small(name)[:, :].rearrange("p (k n) -> p k n", k=4), ACT.Copy).then_inc(act_hi.sem, 1)

            def split_pair(layer, name, dst, q):
                act.wait_ge(small_full.sem, small_full.at(layer, name))
                act.activation(dst[:, 0, 2 * q:2 * q + 2, :],
                                         small(name)[:, :].rearrange("p (k n) -> p k n", k=2), ACT.Copy).then_inc(act_hi.sem, 1)

            def copy_small(layer, name, dst, n):
                act.wait_ge(small_full.sem, small_full.at(layer, name))
                src = small(name)[:, 0:n * P].rearrange("p (k n) -> p k n", k=n)
                act.activation(dst, src, ACT.Copy).then_inc(bank_sem(name), 1)

            def evac_copy(layer, c, dst, func=ACT.Copy):
                act.wait_ge(block_used, chunk_at(layer, c.name))
                act.activation(dst[:, 0], acc(c, 0)[:, :], func)
                act.activation(dst[:, 1], acc(c, 1)[:, :], func).then_inc(acc_free[c.parity].sem, 1)

            def exps(layer, g):
                t, sig = int(g[1]), soft_dve[g]
                nk = P * (t + 1)
                act.wait_ge(sig.sem, sig.at(layer, "shift"))
                for h in range(8):
                    ins = act.activation(scores[:, h, 0:nk], scores[:, h, 0:nk], ACT.Exp, bias=snm[:, h:h + 1],
                                         scale=0.125, accum_out=ssum[:, h:h + 1])
                ins.then_inc(soft_act[g].sem, 1)
                if g[0] == "a":
                    act.wait_ge(sig.sem, sig.at(layer, "sink shift"))
                    act.activation(ses[:, :], sds[:, :], ACT.Exp).then_inc(soft_act[g].sem, 1)

            def relu(layer, name, lo, nk):
                act.wait_ge(small_full.sem, small_full.at(layer, name))
                (act.activation(relu_sb[:, lo:4:2, 0:nk],
                                       small(name)[:, 0:2 * nk].rearrange("p (h n) -> p h n", h=2), ACT.Relu,
                                       scale=0.125)).then_inc(bank_sem(name), 1)

            def probs_copied(layer, g):
                t = int(g[1])
                for i in range(2 * (t + 1)):
                    copy_small(layer, f"p_{g}_{i}", probs_t[:, 4 * i:4 * i + 4, :], 4)

            head_tiles = {"idx": (10, 13, 1), "bq": (0, 4, 1), "kv": (4, 10, 5), "aq": (5, 9, 1), "rqk": (13, 17, 1)}

            def heads_copied(layer, name):
                lo, hi_, by = head_tiles[name]
                for t in range(NT):
                    n = len(range(lo, hi_, by))
                    copy_small(layer, f"tr_{name}{t}", heads_t[:, lo:hi_:by, t * P:(t + 1) * P], n)

            def cross_exps(layer, t):
                act.wait_ge(xsoft_dve.sem, xsoft_dve.at(layer, f"shift{t}"))
                if t:
                    act.wait_ge(small_full.sem, small_full.at(layer, "xp01"))
                for i in range(2):
                    for j in range(2):
                        h = 2 * i + j
                        ins = act.activation(xs_scores[:, h, :], small(f"xs{t}{i}")[:, j * T:(j + 1) * T],
                                             ACT.Exp, bias=snm[:, h:h + 1], scale=0.0625, accum_out=ssum[:, h:h + 1])
                    ins.then_inc(bank_sem(f"xs{t}{i}"), 1)

            def cross_probs(layer, t):
                for i in range(2):
                    copy_small(layer, f"xp{t}{i}", x_probs_t[:, 4 * i:4 * i + 4, :], 4)

            def slot_work(layer, name):
                if name == "pu":
                    evac_copy(layer, CH[name], pu_rv)
                elif name == "idx":
                    for i in range(2):
                        act.wait_ge(small_full.sem, small_full.at(layer, f"pool{i}"))
                        (act.activation(pooled_t[:, 2 * i:2 * i + 2, :],
                                               small(f"pool{i}")[:, :].rearrange("p (g n) -> p g n", g=2), ACT.Copy)).then_inc(bank_sem(f"pool{i}"), 1)
                elif name == "bq":
                    for i in range(2):
                        split_scaled(layer, f"pooly{i}", stat1, [(2 * i, 32 + 2 * i), (2 * i + 1, 33 + 2 * i)])
                    heads_copied(layer, "idx")
                elif name == "kv":
                    heads_copied(layer, "bq")
                    relu(layer, "lg0a", 0, P)
                    relu(layer, "lg0b", 1, P)
                elif name == "aq":
                    heads_copied(layer, "kv")
                    act.wait_ge(weigh.sem, weigh.at(layer, "0 head3"))
                    relu(layer, "lg1a", 0, T)
                    relu(layer, "lg1b", 1, T)
                elif name == "rqk":
                    heads_copied(layer, "aq")
                elif name == "rv":
                    evac_copy(layer, CH[name], pu_rv)
                    heads_copied(layer, "rqk")
                elif name == "rg":
                    evac_copy(layer, CH[name], rg, ACT.Silu)
                elif name.startswith("gate"):
                    if name != "gateD0":
                        prev = {"D1": "D0", "C0": "D1", "C1": "C0", "A0": "C1", "A1": "A0", "B0": "A1", "B1": "B0"}[name[4:]]
                        if prev[0] == "D":
                            act.wait_ge(acc_free[1].sem, acc_free[1].at(layer, f"up{prev}"))
                        else:
                            act.wait_ge(up_added.sem, up_added.at(layer, prev))
                    evac_copy(layer, CH[name], gate, ACT.Sigmoid)
                if name == "gateD0":
                    exps(layer, "a0")
                    for t in range(NT):
                        act.wait_ge(small_full.sem, small_full.at(layer, f"ro{t}"))
                        for h in range(4):
                            ins = act.activation(roped[:, t, h * P:(h + 1) * P], small(f"ro{t}")[:, h * P:(h + 1) * P], ACT.Square,
                                                 accum_out=rss[:, t, h:h + 1])
                    ins.then_inc(ret_act.sem, 1)
                    act.wait_ge(ret_act.sem, ret_act.at(layer, "squares"))
                    act.activation(rrt[:, :, :], rss[:, :, :], ACT.Sqrt, bias=eps_sb[:, 0:1], scale=1.0 / P).then_inc(ret_act.sem, 1)
                elif name == "upD0":
                    act.wait_ge(weigh.sem, weigh.at(layer, "1 head3"))
                    probs_copied(layer, "a0")
                elif name == "upD1":
                    for t in range(NT):
                        split_rows(layer, f"tC{t}", stat1[:, 0, 4:8, :], t)
                elif name == "gateC0":
                    exps(layer, "a1")
                elif name == "upC0":
                    act.wait_ge(small_full.sem, small_full.at(layer, "o_a0"))
                    probs_copied(layer, "a1")
                elif name == "gateC1":
                    exps(layer, "b0")
                elif name == "upC1":
                    for t in range(NT):
                        split_rows(layer, f"tA{t}", stat1[:, 0, 0:4, :], t)
                    act.wait_ge(small_full.sem, small_full.at(layer, "o_a1"))
                    probs_copied(layer, "b0")
                elif name == "gateA0":
                    exps(layer, "b1")
                elif name == "upA0":
                    act.wait_ge(small_full.sem, small_full.at(layer, "o_b0"))
                    probs_copied(layer, "b1")
                elif name == "gateB0":
                    for t in range(NT):
                        split_rows(layer, f"tB{t}", stat1[:, 0, 4:8, :], t)
                elif name == "upB1":
                    for q in range(4):
                        split_pair(layer, f"m{q}", stat0, q)
                    for k in range(KD):
                        ins = act.activation(stat1[:, 0, k, :], memT[:, k, :], ACT.Copy, scale=gn[:, 16 + k:17 + k])
                    ins.then_inc(act_hi.sem, 1)
                elif name == "out1":
                    act.wait_ge(acc_free[1].sem, acc_free[1].at(layer, "out1"))
                    norm(layer, norm_act, norm_dve, "cross ", x, tok)
                elif name in ("xkv0", "xkv1"):
                    evac_copy(layer, CH[name], k_tok[:, :, int(name[3]) * 512:(int(name[3]) + 1) * 512])
                    if name == "xkv1":
                        for q in range(4):
                            split_scaled(layer, f"c{q}", stat0, [(2 * q, 8 + 2 * q), (2 * q + 1, 9 + 2 * q)])
                elif name in ("xkv2", "xkv3"):
                    evac_copy(layer, CH[name], v_tok[:, :, (int(name[3]) - 2) * 512:(int(name[3]) - 1) * 512])
                elif name in ("xq0", "xq1"):
                    evac_copy(layer, CH[name], q_tok[:, :, int(name[2]) * 512:(int(name[2]) + 1) * 512])
                if name == "xkv2":
                    for q in range(4):
                        act.wait_ge(small_full.sem, small_full.at(layer, f"xq{q}"))
                        (act.activation(qT_x[:, 2 * q:2 * q + 2, :],
                                               small(f"xq{q}")[:, :].rearrange("p (k n) -> p k n", k=2), ACT.Copy)).then_inc(bank_sem(f"xq{q}"), 1)
                    cross_exps(layer, 0)
                elif name == "xkv3":
                    cross_probs(layer, 0)
                    cross_exps(layer, 1)
                    act.wait_ge(small_full.sem, small_full.at(layer, "xo01"))
                    cross_probs(layer, 1)
                    for q in range(4):
                        split_pair(layer, f"xt{q}", stat1, q)
                elif name == "xo1":
                    act.wait_ge(acc_free[1].sem, acc_free[1].at(layer, "xo1"))
                    norm(layer, norm_act, norm_dve, "ffn ", x, tok)
                    for q in range(4):
                        split_scaled(layer, f"f{q}", stat0, [(2 * q, 24 + 2 * q), (2 * q + 1, 25 + 2 * q)])

            def feed_forward(base, first, kind, job=None):
                tiles = NT if kind == 0 else 1
                s_tr, s_silu, s_hid, s_hi = ffn_tr[kind], ffn_silu[kind], ffn_hid[kind], ffn_hi[kind]
                high = expert_hi if kind else hi

                def silu(u):
                    act.wait_ge(block_used, used_at(plus(gu_block(base, u), 1)))
                    if not (isinstance(u, int) and u == 0):
                        act.wait_ge(s_hid.sem, s_hid.at(first + (u - 1), "hid"))
                    for t in range(tiles):
                        ins = act.activation(silu_g[:, t, :], bank[t][:, :], ACT.Silu)
                    ins.then_inc(s_silu.sem, 1)

                def transposed(u):
                    act.wait_ge(s_tr.sem, s_tr.at(first + u, "tr"))
                    for t in range(tiles):
                        src = bank[(4 if kind == 0 else 2) + t][:, :].rearrange("p (k n) -> p k n", k=4)
                        ins = act.activation(stat1[:, 0, 0:4, t * P:(t + 1) * P], src, ACT.Copy)
                    ins.then_inc(s_hi.sem, 1)

                def body(u, last):
                    gu, dn = gu_block(base, u), down_block(base, u - 1)
                    high(plus(gu, 1))
                    high(plus(gu, 2))
                    high(plus(gu, 3))
                    transposed(u - 1)
                    high(dn)
                    silu(u)
                    high(plus(dn, 1))
                    if not last:
                        high(gu_block(base, u + 1))

                gu = gu_block(base, 0)
                high(gu)
                if kind:
                    rows_out(job)
                for j in (1, 2):
                    high(plus(gu, j))
                high(plus(gu, 3))
                silu(0)
                high(plus(gu, 4))
                body(1, False)
                if kind:
                    picks(job)
                with act.Fori(2, UNITS - 1) as u:
                    body(u, False)
                body(UNITS - 1, True)
                dn = down_block(base, UNITS - 1)
                high(dn)
                high(plus(dn, 1))
                transposed(UNITS - 1)

            def gathered(j):
                for i, step in enumerate(("low", "high")):
                    act.wait_ge(gather_full.sem, gather_full.at(j, step))
                    for k in range(4):
                        col = 24 + 4 * i + k
                        ins = act.activation(stat0[:, 0, 4 * i + k, 0:P], bank[4 + i][:, k * P:(k + 1) * P], ACT.Copy,
                                             scale=gn[:, col:col + 1])
                    ins.then_inc(gather_hi.sem, 1)

            def rows_out(j):
                act.wait_ge(block_used, number((job_base(j), 0)) + SPLIT_SLOTS)
                for i in range(2):
                    ins = act.activation(y_sb[:, i * 512:(i + 1) * 512], bank[6 + i][:, :], ACT.Copy)
                ins.then_inc(y_copied.sem, 1)

            def picks(j):
                act.wait_ge(picks_full.sem, picks_full.at(j, "picks"))
                act.activation(wpick_t, bank[3][:, 0:T].rearrange("p (t n) -> p t n", t=NT), ACT.Copy).then_inc(picks_copied.sem, 1)

            with act.Fori(0, DEPTH) as layer:
                hi_chunk(layer, CHUNKS[0])
                act.wait_ge(layer_consts.sem, layer_consts.at(layer, "sinks"))
                act.wait_ge(setup_full, 5)
                norm(layer, norm_act, norm_dve, "mix ", x, tok)
                for q in range(4):
                    split_scaled(layer, f"h{q}", stat0, [(2 * q, 2 * q), (2 * q + 1, 2 * q + 1)])
                for c, after in zip(CHUNKS, CHUNKS[1:] + [None]):
                    if after is not None:
                        hi_chunk(layer, after)
                    slot_work(layer, c.name)
                with act.If(layer == 0):
                    feed_forward(DENSE_BASE, 0, 0)
                with act.Else():
                    act.wait_ge(route_dve, ROUTE_DIFF)
                    act.activation(rt_exp, rt_diff, ACT.Exp).then_inc(route_act, 1)
                    gathered(0)
                    act.wait_ge(routed, 1)
                    n_jobs = act.value_load(route_i[0:1, 3:4], min_val=0, max_val=3) + E
                    with act.Fori(0, n_jobs) as j:
                        feed_forward(job_base(j), j * UNITS, 1, j)
                        gathered(j + 1)
                    rows_out(n_jobs)
                act.nop()
            act.wait_ge(x_stands, 1)
            norm(1, ends_act, ends_dve, "", x, tok)

        @block.vector
        def _(dve):
            def lo(b, width=UNIT):
                dve.wait_ge(hi_done, number(b) + 1)
                dve.tensor_tensor(w_lo[:, slot(b), :, 0:width], raw[:, slot(b), :, 0:width],
                                  f32_of(w_hi[:, slot(b), :, 0:width]), ALU.subtract).then_inc(lo_done, 1)

            def expert_lo(b):
                dve.wait_ge(hi_done, number(b) + 1)
                dve.tensor_tensor(w_lo[:, slot(b), :, :], expert_raw[expert_slot(b)],
                                  f32_of(w_hi[:, slot(b), :, :]), ALU.subtract).then_inc(lo_done, 1)

            def lo_chunk(layer, c):
                for i in range(c.blocks):
                    lo(chunk_block(layer, c, i), c.n)

            def norm(turn, sig, act_sig, pre, src, dst):
                dve.scalar_tensor_tensor(out=dst[:, 1, :], in0=src[:, 1, :], scalar=1.0, in1=src[:, 1, :],
                                                op0=ALU.mult, op1=ALU.mult, accum_out=ss[:, 1:2]).then_inc(sig.sem, 1)
                dve.wait_ge(act_sig.sem, act_sig.at(turn, f"{pre}root"))
                dve.reciprocal(rs[:, :], rt[:, :]).then_inc(sig.sem, 1)
                dve.wait_ge(sig.sem, sig.at(turn, f"{pre}inv"))
                dve.tensor_scalar(dst[:, 1, :], src[:, 1, :], rs[:, 1:2], None, ALU.mult).then_inc(sig.sem, 1)

            made = [0]

            def link(ins, s=trig_dve):
                made[0] += 1
                ins.then_inc(s, 1)
                dve.wait_ge(s, made[0])

            dve.sem_inc(lo_done, RAW_SLOTS)
            dve.wait_ge(inputs_landed, 16 * N_SMALL_LOADS)
            dve.wait_ge(consts_ready, 1)
            norm(0, ends_dve, ends_act, "", tok, k_tok)
            link(dve.tensor_copy(pos_f[:, :], pos_i[:, :]))
            for t in range(NT):
                link(dve.tensor_scalar(ang[:, t, :], inv_freq, pos_f[:, t:t + 1], None, ALU.mult))
            link(dve.tensor_scalar(turns_i, ang, 1.0 / TWO_PI, None, ALU.mult))
            link(dve.tensor_copy(turns_f, turns_i))
            link(dve.scalar_tensor_tensor(out=red, in0=turns_f, scalar=-PI2_A, in1=ang, op0=ALU.mult, op1=ALU.add))
            link(dve.scalar_tensor_tensor(out=red, in0=turns_f, scalar=-PI2_B, in1=red, op0=ALU.mult, op1=ALU.add))
            link(dve.scalar_tensor_tensor(out=red, in0=turns_f, scalar=-PI2_C, in1=red, op0=ALU.mult, op1=ALU.add))

            def wrap(r):
                for op, edge, by in ((ALU.is_gt, math.pi, -TWO_PI), (ALU.is_lt, -math.pi, TWO_PI)):
                    link(dve.tensor_scalar(over, r, edge, by, op, ALU.mult))
                    link(dve.tensor_tensor(r, r, over, ALU.add))
                link(dve.tensor_scalar(r, r, 3.1415925, -3.1415925, ALU.min, ALU.max))

            link(dve.tensor_scalar(red2, red, math.pi / 2, None, ALU.add))
            wrap(red)
            wrap(red2)
            assert made[0] == TRIG_REDUCED, made
            dve.wait_ge(setup_full, 1)
            dve.tensor_copy(gains[:, :], bank[0][:, 0:72]).then_inc(setup_free, 1)

            def take_layer_constants(l):
                dve.tensor_copy(gn[:, 0:32].rearrange("p (k j) -> p k j", k=4),
                                                gains[:, 0:64].rearrange("p (k l j) -> p k l j", k=4, l=2)[:, :, l, :]).then_inc(layer_consts.sem, 1)
                dve.tensor_copy(gn[:, 32:36], gains[:, 64 + 4 * l:68 + 4 * l]).then_inc(layer_consts.sem, 1)
                dve.tensor_copy(sink_now[:, :], sink_sb[:, l, :]).then_inc(layer_consts.sem, 1)

            dve.wait_ge(setup_free, 1)
            take_layer_constants(0)
            for q in range(4):
                dve.wait_ge(setup_full, q + 2)
                dve.tensor_copy(memT[:, 2 * q:2 * q + 2, :],
                                bank[4 + q][:, :].rearrange("p (k n) -> p k n", k=2)).then_inc(setup_free, 1)
            dve.wait_ge(setup_split, 1)
            dve.tensor_tensor(rw_lo[:, :, :], rw[:, :, :], f32_of(rw_hi[:, :, :]), ALU.subtract)
            dve.wait_ge(consts_ready, 3)
            dve.wait_ge(trig_step, TRIG_SINES)

            def split_scaled(layer, name, dst, pairs):
                dve.wait_ge(act_hi.sem, act_hi.at(layer, name))
                for i, (k, col) in enumerate(pairs):
                    ins = dve.scalar_tensor_tensor(out=dst[:, 1, k, :], in0=small(name)[:, i * T:(i + 1) * T],
                                                   scalar=gn[:, col:col + 1], in1=f32_of(dst[:, 0, k, :]),
                                                   op0=ALU.mult, op1=ALU.subtract)
                ins.then_inc(bank_sem(name), 1)

            def split_rows(layer, name, k0, t):
                dve.wait_ge(act_hi.sem, act_hi.at(layer, name))
                cols = slice(t * P, (t + 1) * P)
                (dve.tensor_tensor(stat1[:, 1, k0:k0 + 4, cols],
                                          small(name)[:, :].rearrange("p (k n) -> p k n", k=4),
                                          f32_of(stat1[:, 0, k0:k0 + 4, cols]), ALU.subtract)).then_inc(bank_sem(name), 1)

            def split_pair(layer, name, dst, q):
                dve.wait_ge(act_hi.sem, act_hi.at(layer, name))
                (dve.tensor_tensor(dst[:, 1, 2 * q:2 * q + 2, :],
                                          small(name)[:, :].rearrange("p (k n) -> p k n", k=2),
                                          f32_of(dst[:, 0, 2 * q:2 * q + 2, :]), ALU.subtract)).then_inc(bank_sem(name), 1)

            def rotate(layer, name):
                c = CH[name]
                dve.wait_ge(block_used, chunk_at(layer, name))
                for t in range(NT):
                    n = ROPE_CHUNKS.index(name)
                    if n:
                        dve.wait_ge(rope_add.sem, rope_add.at(layer, f"{ROPE_CHUNKS[n - 1]}{t}"))
                    src = acc(c, t)
                    parts = [(0, 0, 2), (128, 256, 2)] if name == "kv" else [(0, 0, 5 if name == "idx" else 8)]
                    for dst_at, src_at, h in parts:
                        v = src[:, src_at:src_at + h * 64].rearrange("p (h s d) -> p h s d", h=h, s=2)
                        r1 = rope1[:, t, dst_at:dst_at + h * 64].rearrange("p (h d) -> p h d", h=h)
                        r2 = rope2[:, t, dst_at:dst_at + h * 64].rearrange("p (h s d) -> p h s d", h=h, s=2)
                        dve.tensor_tensor(r2[:, :, 0, :], v[:, :, 1, :], nsin1[:, t:t + 1, :].broadcast_to([P, h, 32]),
                                          ALU.mult)
                        dve.tensor_tensor(r2[:, :, 1, :], v[:, :, 0, :], sin1[:, t:t + 1, :].broadcast_to([P, h, 32]),
                                          ALU.mult)
                        ins = dve.tensor_tensor(r1, src[:, src_at:src_at + h * 64].rearrange("p (h d) -> p h d", h=h),
                                                cos2[:, t:t + 1, :].broadcast_to([P, h, 64]), ALU.mult)
                    ins.then_inc(rope_mult.sem, 1)
                if name == "idx":
                    for t in range(NT):
                        ins = dve.tensor_scalar(iw[:, t, :], acc(c, t)[:, 320:324], 0.5, None, ALU.mult)
                    ins.then_inc(acc_free[c.parity].sem, 1)
                if name == "kv":
                    for t in range(NT):
                        ins = dve.tensor_copy(v_ab[:, t, :, :],
                                              acc(c, t)[:, :].rearrange("p (g n) -> p g n", g=2)[:, :, 128:256])
                    ins.then_inc(acc_free[c.parity].sem, 1)

            def select(layer, t):
                nk = P * (t + 1)
                w = work[:, 0:nk]
                causal = mask_c[:, T - nk:T]
                dve.wait_ge(bank_sem("lg1b" if t else "lg0b"), emptied_at(layer, "lg1b" if t else "lg0b"))
                dve.wait_ge(acc_free[CH["idx"].parity].sem, acc_free[CH["idx"].parity].at(layer, "idx"))
                for h in range(4):
                    if h == 0:
                        ins = dve.tensor_scalar(w, relu_sb[:, 0, 0:nk], iw[:, t, 0:1], None, ALU.mult)
                    else:
                        ins = dve.scalar_tensor_tensor(out=w, in0=relu_sb[:, h, 0:nk], scalar=iw[:, t, h:h + 1], in1=w,
                                                       op0=ALU.mult, op1=ALU.add)
                    ins.then_inc(weigh.sem, 1)
                    dve.wait_ge(weigh.sem, weigh.at(layer, f"{t} head{h}"))
                dve.tensor_tensor(w, w, causal, ALU.add).then_inc(rank.sem, 1)
                last = f"{t} causal"
                for i in range(N_SEL // 8):
                    dve.wait_ge(rank.sem, rank.at(layer, last))
                    dve.sem_inc(rank_alone, 1)
                    last = f"{t} top{i}"
                    dve.max(top8[:, :], w).then_inc(rank.sem, 1)
                    dve.wait_ge(rank.sem, rank.at(layer, last))
                    dve.sem_inc(rank_alone, 1)
                    last = f"{t} take{i}"
                    dve.match_replace(out=w, in_to_replace=top8[:, :], in_values=w, imm_value=TAKEN).then_inc(rank.sem, 1)
                dve.wait_ge(rank.sem, rank.at(layer, last))
                m = sel_mask[:, t, 0:nk]
                dve.tensor_scalar(m, w, -2.0e38, NEG, ALU.is_gt, ALU.mult).then_inc(rank.sem, 1)
                dve.wait_ge(rank.sem, rank.at(layer, f"{t} left"))
                dve.tensor_tensor(m, m, causal, ALU.add).then_inc(rank.sem, 1)

            def soft_start(layer, g):
                t, sig = int(g[1]), soft_dve[g]
                nk, banks = P * (t + 1), 2 * (t + 1)
                if g == "a0":
                    dve.wait_ge(rope_add.sem, rope_add.at(layer, "rqk1"))
                else:
                    before = GROUPS[GROUPS.index(g) - 1]
                    dve.wait_ge(small_full.sem, small_full.at(layer, f"p_{before}_{2 * (int(before[1]) + 1) - 1}"))
                if g[0] == "a":
                    mask = mask_a[:, :] if t else mask_c[:, P:T]
                else:
                    dve.wait_ge(rank.sem, rank.at(layer, f"{t} mask"))
                    mask = sel_mask[:, t, 0:nk]
                hn = 8 // banks
                for i in range(banks):
                    name = f"s_{g}_{i}"
                    dve.wait_ge(small_full.sem, small_full.at(layer, name))
                    (dve.tensor_tensor(scores[:, i * hn:(i + 1) * hn, 0:nk],
                                              small(name)[:, :].rearrange("p (h n) -> p h n", h=hn),
                                              mask.rearrange("p (a n) -> p a n", a=1).broadcast_to([P, hn, nk]),
                                              ALU.add)).then_inc(bank_sem(name), 1)
                for i in range(max(0, banks - 4), banks):
                    dve.wait_ge(bank_sem(f"s_{g}_{i}"), emptied_at(layer, f"s_{g}_{i}"))
                dve.tensor_reduce(smx[:, :], scores[:, :, 0:nk], AX.X, ALU.max).then_inc(sig.sem, 1)
                dve.wait_ge(sig.sem, sig.at(layer, "max"))
                if g[0] == "a":
                    dve.scalar_tensor_tensor(out=sm[:, :], in0=smx[:, :], scalar=0.125, in1=sink_now[:, :],
                                                    op0=ALU.mult, op1=ALU.max).then_inc(sig.sem, 1)
                    dve.wait_ge(sig.sem, sig.at(layer, "sunk"))
                    dve.tensor_scalar(snm[:, :], sm[:, :], -1.0, None, ALU.mult).then_inc(sig.sem, 1)
                    dve.tensor_tensor(sds[:, :], sink_now[:, :], sm[:, :], ALU.subtract).then_inc(sig.sem, 1)
                else:
                    dve.tensor_scalar(snm[:, :], smx[:, :], -0.125, None, ALU.mult).then_inc(sig.sem, 1)

            def soft_end(layer, g):
                sig = soft_dve[g]
                if g[0] == "a":
                    dve.wait_ge(soft_act[g].sem, soft_act[g].at(layer, "sink exp"))
                    dve.tensor_tensor(ssum[:, :], ssum[:, :], ses[:, :], ALU.add).then_inc(sig.sem, 1)
                    dve.wait_ge(sig.sem, sig.at(layer, "total"))
                else:
                    dve.wait_ge(soft_act[g].sem, soft_act[g].at(layer, "exp"))
                dve.reciprocal(sinv[:, :], ssum[:, :]).then_inc(sig.sem, 1)

            def soft_out(layer, g):
                name = f"o_{g}"
                dve.wait_ge(soft_dve[g].sem, soft_dve[g].at(layer, "inv"))
                dve.wait_ge(small_full.sem, small_full.at(layer, name))
                if g[0] == "b":
                    dve.wait_ge(small_full.sem, small_full.at(layer, "tC1"))
                dst = o_buf[:, 1 if g[0] == "a" else 0, int(g[1]), :]
                (dve.tensor_tensor(heads(dst, 8), heads(small(name)[:, :], 8),
                                          sinv[:, :].rearrange("p (h a) -> p h a", a=1).broadcast_to([P, 8, 64]),
                                          ALU.mult)).then_inc(bank_sem(name), 1)

            def gated(layer, name):
                branch, half, c = name[2], int(name[3]), CH[name]
                cols = slice(half * 512, (half + 1) * 512)
                dve.wait_ge(acc_free[CH[f"gate{branch}{half}"].parity].sem, acc_free[CH[f"gate{branch}{half}"].parity].at(layer, f"gate{branch}{half}"))
                dve.wait_ge(block_used, chunk_at(layer, name))
                for t in range(NT):
                    dst = merged[:, t, cols] if branch == "D" else gate[:, t, :]
                    ins = dve.tensor_tensor(dst, acc(c, t)[:, :], gate[:, t, :], ALU.mult)
                ins.then_inc(acc_free[c.parity].sem, 1)
                dve.wait_ge(acc_free[c.parity].sem, acc_free[c.parity].at(layer, name))
                if branch != "D":
                    dve.tensor_tensor(merged[:, :, cols], merged[:, :, cols], gate[:, :, :], ALU.add).then_inc(up_added.sem, 1)

            def residual(layer, name):
                c, half = CH[name], int(name[-1])
                dve.wait_ge(block_used, chunk_at(layer, name))
                for t in range(NT):
                    xs = x[:, t, half * 512:(half + 1) * 512]
                    ins = dve.tensor_tensor(xs, xs, acc(c, t)[:, :], ALU.add)
                ins.then_inc(acc_free[c.parity].sem, 1)

            def cross_start(layer, t):
                for i in range(2):
                    dve.wait_ge(small_full.sem, small_full.at(layer, f"xs{t}{i}"))
                    ins = dve.tensor_reduce(smx[:, 2 * i:2 * i + 2],
                                            small(f"xs{t}{i}")[:, :].rearrange("p (h n) -> p h n", h=2), AX.X, ALU.max)
                ins.then_inc(xsoft_dve.sem, 1)
                dve.wait_ge(xsoft_dve.sem, xsoft_dve.at(layer, f"max{t}"))
                dve.tensor_scalar(snm[:, 0:4], smx[:, 0:4], -0.0625, None, ALU.mult).then_inc(xsoft_dve.sem, 1)

            def cross_inv(layer, t):
                dve.wait_ge(bank_sem(f"xs{t}1"), emptied_at(layer, f"xs{t}1"))
                dve.reciprocal(sinv[:, 4 * t:4 * t + 4], ssum[:, 0:4]).then_inc(xsoft_dve.sem, 1)

            def cross_out(layer, t):
                dve.wait_ge(xsoft_dve.sem, xsoft_dve.at(layer, f"inv{t}"))
                for i in range(2):
                    name = f"xo{t}{i}"
                    dve.wait_ge(small_full.sem, small_full.at(layer, name))
                    (dve.tensor_tensor(
                        tok[:, t, i * 512:(i + 1) * 512].rearrange("p (h n) -> p h n", h=2),
                        small(name)[:, :].rearrange("p (h n) -> p h n", h=2),
                        sinv[:, 4 * t + 2 * i:4 * t + 2 * i + 2].rearrange("p (h a) -> p h a", a=1).broadcast_to([P, 2, T]),
                        ALU.mult)).then_inc(bank_sem(name), 1)

            def slot_work(layer, name):
                if name in ROPE_CHUNKS:
                    rotate(layer, name)
                if name == "bq":
                    for i in range(2):
                        split_scaled(layer, f"pooly{i}", stat1, [(2 * i, 32 + 2 * i), (2 * i + 1, 33 + 2 * i)])
                elif name == "aq":
                    select(layer, 0)
                elif name == "rqk":
                    select(layer, 1)
                elif name == "rv":
                    soft_start(layer, "a0")
                elif name == "rg":
                    for h in range(4):
                        s, b = f"st{h}", small(f"st{h}")
                        dve.wait_ge(small_full.sem, small_full.at(layer, s))
                        dve.tensor_tensor(decayed[:, h, 0:T], b[:, 0:T], decay[:, h, :], ALU.mult)
                        dve.tensor_tensor(decayed[:, h, T:T + P], b[:, T:T + P], decay[:, h, 0:P], ALU.mult).then_inc(bank_sem(s), 1)
                elif name == "gateD0":
                    soft_end(layer, "a0")
                    dve.wait_ge(ret_act.sem, ret_act.at(layer, "root"))
                    dve.reciprocal(rrs[:, :, :], rrt[:, :, :]).then_inc(ret_dve.sem, 1)
                    dve.wait_ge(ret_dve.sem, ret_dve.at(layer, "inv"))
                    dve.wait_ge(acc_free[CH["rg"].parity].sem, acc_free[CH["rg"].parity].at(layer, "rg"))
                    for t in range(NT):
                        for h in range(4):
                            cols = slice(h * P, (h + 1) * P)
                            ins = dve.scalar_tensor_tensor(out=o_buf[:, 0, t, cols], in0=small(f"ro{t}")[:, cols],
                                                           scalar=rrs[:, t, h:h + 1], in1=rg[:, t, cols],
                                                           op0=ALU.mult, op1=ALU.mult)
                        ins.then_inc(bank_sem(f"ro{t}"), 1)
                elif name.startswith("up"):
                    gated(layer, name)
                if name == "gateD1":
                    soft_out(layer, "a0")
                elif name == "upD1":
                    for t in range(NT):
                        split_rows(layer, f"tC{t}", 4, t)
                elif name == "gateC0":
                    soft_start(layer, "a1")
                    soft_end(layer, "a1")
                elif name == "gateC1":
                    soft_out(layer, "a1")
                    soft_start(layer, "b0")
                    soft_end(layer, "b0")
                elif name == "upC1":
                    for t in range(NT):
                        split_rows(layer, f"tA{t}", 0, t)
                elif name == "gateA0":
                    soft_out(layer, "b0")
                    soft_start(layer, "b1")
                    soft_end(layer, "b1")
                elif name == "gateA1":
                    soft_out(layer, "b1")
                elif name == "gateB0":
                    for t in range(NT):
                        split_rows(layer, f"tB{t}", 4, t)
                elif name == "upB1":
                    for q in range(4):
                        split_pair(layer, f"m{q}", stat0, q)
                    dve.wait_ge(act_hi.sem, act_hi.at(layer, "mem"))
                    for k in range(KD):
                        ins = dve.scalar_tensor_tensor(out=stat1[:, 1, k, :], in0=memT[:, k, :],
                                                       scalar=gn[:, 16 + k:17 + k], in1=f32_of(stat1[:, 0, k, :]),
                                                       op0=ALU.mult, op1=ALU.subtract)
                    ins.then_inc(mem_split.sem, 1)
                elif name in ("out0", "out1"):
                    residual(layer, name)
                    if name == "out1":
                        dve.wait_ge(acc_free[CH[name].parity].sem, acc_free[CH[name].parity].at(layer, name))
                        norm(layer, norm_dve, norm_act, "cross ", x, tok)
                elif name == "xkv1":
                    for q in range(4):
                        split_scaled(layer, f"c{q}", stat0, [(2 * q, 8 + 2 * q), (2 * q + 1, 9 + 2 * q)])
                elif name == "xq0":
                    for q in range(4):
                        dve.wait_ge(small_full.sem, small_full.at(layer, f"xk{q}"))
                        (dve.tensor_copy(kT_x[:, 2 * q:2 * q + 2, :],
                                                small(f"xk{q}")[:, :].rearrange("p (k n) -> p k n", k=2))).then_inc(bank_sem(f"xk{q}"), 1)
                elif name == "xkv2":
                    cross_start(layer, 0)
                    cross_inv(layer, 0)
                elif name == "xkv3":
                    cross_start(layer, 1)
                    cross_inv(layer, 1)
                    cross_out(layer, 0)
                    cross_out(layer, 1)
                    for q in range(4):
                        split_pair(layer, f"xt{q}", stat1, q)
                elif name in ("xo0", "xo1"):
                    residual(layer, name)
                    if name == "xo1":
                        dve.wait_ge(acc_free[CH[name].parity].sem, acc_free[CH[name].parity].at(layer, name))
                        norm(layer, norm_dve, norm_act, "ffn ", x, tok)
                        for q in range(4):
                            split_scaled(layer, f"f{q}", stat0, [(2 * q, 24 + 2 * q), (2 * q + 1, 25 + 2 * q)])

            def feed_forward(base, first, kind, job=None):
                tiles = NT if kind == 0 else 1
                s_tr, s_silu, s_hid, s_hi, s_lo = (s[kind] for s in (ffn_tr, ffn_silu, ffn_hid, ffn_hi, ffn_lo))
                low = expert_lo if kind else lo

                def hidden(u):
                    dve.wait_ge(s_silu.sem, s_silu.at(first + u, "silu"))
                    dve.wait_ge(block_used, used_at(plus(gu_block(base, u), 3)))
                    if not (isinstance(u, int) and u == 0):
                        dve.wait_ge(s_tr.sem, s_tr.at(first + (u - 1), "tr"))
                    for t in range(tiles):
                        ins = dve.tensor_tensor(hid[:, t, :], bank[tiles + t][:, :], silu_g[:, t, :], ALU.mult)
                    ins.then_inc(s_hid.sem, 1)

                def transposed(u):
                    dve.wait_ge(s_hi.sem, s_hi.at(first + u, "hi"))
                    for t in range(tiles):
                        cols = slice(t * P, (t + 1) * P)
                        src = bank[(4 if kind == 0 else 2) + t][:, :].rearrange("p (k n) -> p k n", k=4)
                        ins = dve.tensor_tensor(stat1[:, 1, 0:4, cols], src, f32_of(stat1[:, 0, 0:4, cols]), ALU.subtract)
                    ins.then_inc(s_lo.sem, 1)

                def add_half(u, half):
                    if kind:
                        return
                    dve.wait_ge(block_used, used_at(plus(down_block(base, u), half)))
                    for t in range(NT):
                        xs = x[:, t, half * 512:(half + 1) * 512]
                        ins = dve.tensor_tensor(xs, xs, bank[(6 if half == 0 else 4) + t][:, :], ALU.add)
                    ins.then_inc(ffn_acc.sem, 1)

                def body(u, last):
                    gu, dn = gu_block(base, u), down_block(base, u - 1)
                    hidden(u - 1)
                    low(plus(gu, 1))
                    low(plus(gu, 2))
                    low(plus(gu, 3))
                    transposed(u - 1)
                    low(dn)
                    low(plus(dn, 1))
                    add_half(u - 1, 0)
                    if not last:
                        low(gu_block(base, u + 1))
                    add_half(u - 1, 1)

                gu = gu_block(base, 0)
                for j in range(5):
                    low(plus(gu, j))
                if kind:
                    scattered(job)
                body(1, False)
                if kind:
                    dve.wait_ge(picks_full.sem, picks_full.at(job, "picks"))
                    pick_slots(job + 1)
                with dve.Fori(2, UNITS - 1) as u:
                    body(u, False)
                body(UNITS - 1, True)
                dn = down_block(base, UNITS - 1)
                hidden(UNITS - 1)
                low(dn)
                low(plus(dn, 1))
                transposed(UNITS - 1)
                add_half(UNITS - 1, 0)
                add_half(UNITS - 1, 1)

            def scattered(j):
                for t in range(NT):
                    dve.wait_ge(scatter_full.sem, scatter_full.at(j, f"t{t}"))
                    for half in range(2):
                        xs = x[:, t, half * 512:(half + 1) * 512]
                        ins = dve.tensor_tensor(xs, xs, bank[(4 if t == 0 else 2) + half][:, :], ALU.add)
                    ins.then_inc(scatter_added.sem, 1)

            def pick_slots(j):
                for t in range(NT):
                    ins = dve.tensor_scalar(pick[:, t, :], slots_iota[:, :], slot_of[:, t, bass.ds(j, 1)], None, ALU.is_equal)
                ins.then_inc(pick_ready.sem, 1)
                for t in range(NT):
                    ins = dve.tensor_scalar(wpick[:, t, :], slots_iota[:, :], slot_of[:, t, bass.ds(j, 1)],
                                            gate_of[:, t, bass.ds(j, 1)], ALU.is_equal, ALU.mult)
                ins.then_inc(pick_ready.sem, 1)

            def gathered(j):
                for i, step in enumerate(("low", "high")):
                    dve.wait_ge(gather_hi.sem, gather_hi.at(j, step))
                    for k in range(4):
                        kt = 4 * i + k
                        ins = dve.scalar_tensor_tensor(out=stat0[:, 1, kt, 0:P], in0=bank[4 + i][:, k * P:(k + 1) * P],
                                                       scalar=gn[:, 24 + kt:25 + kt], in1=f32_of(stat0[:, 0, kt, 0:P]),
                                                       op0=ALU.mult, op1=ALU.subtract)
                    ins.then_inc(gather_lo.sem, 1)

            def route():
                made[0] = 0
                step = lambda ins: link(ins, route_dve)
                logits, top, idx, idx_f = (rt_area[:, a:a + 16].rearrange("p (t e) -> p t e", t=NT) for a in (0, 16, 32, 48))
                one1, one2, member, gates = (rt_area[:, a:a + 16].rearrange("p (t e) -> p t e", t=NT) for a in (64, 80, 96, 112))
                w1c, w2c = (rt_area[:, a:a + 2] for a in (128, 130))
                places, junk = (rt_area[:, a:a + 16].rearrange("p (t e) -> p t e", t=NT) for a in (144, 160))
                count, over_e, incl, before, sel = (rt_area[:, a:a + 8] for a in (176, 184, 192, 200, 208))
                cnt_k, none_k, ids = rt_area[:, 216:219], rt_area[:, 220:223], rt_area[:, 224:228]
                s_k = rt_area[:, 232:238].rearrange("p (k t) -> p k t", k=3)
                dve.wait_ge(route_full, 1)
                step(dve.tensor_copy(logits, bank[0][:, 0:16].rearrange("p (t e) -> p t e", t=NT)))
                for t in range(NT):
                    step(dve.max(top[:, t, :], logits[:, t, :]))
                    step(dve.max_index(idx[:, t, :].bitcast(U32), top[:, t, :], logits[:, t, :]))
                step(dve.tensor_tensor(rt_diff, top[:, :, 1], top[:, :, 0], ALU.subtract))
                assert made[0] == ROUTE_DIFF, made
                step(dve.tensor_copy(idx_f, idx.bitcast(U32)))
                dve.wait_ge(route_act, 1)
                step(dve.tensor_scalar(w1c, rt_exp, 1.0, None, ALU.add))
                step(dve.reciprocal(w1c, w1c))
                step(dve.tensor_tensor(w2c, w1c, rt_exp, ALU.mult))
                for t in range(NT):
                    lane = slots_iota[:, 0:8]
                    step(dve.tensor_scalar(one1[:, t, :], lane, idx_f[:, t, 0:1], None, ALU.is_equal))
                    step(dve.tensor_scalar(one2[:, t, :], lane, idx_f[:, t, 1:2], None, ALU.is_equal))
                    step(dve.tensor_scalar(gates[:, t, :], one1[:, t, :], w1c[:, t:t + 1], None, ALU.mult))
                    step(dve.scalar_tensor_tensor(out=gates[:, t, :], in0=one2[:, t, :], scalar=w2c[:, t:t + 1],
                                                  in1=gates[:, t, :], op0=ALU.mult, op1=ALU.add))
                step(dve.tensor_tensor(member, one1, one2, ALU.add))
                assert made[0] == ROUTE_MEMBER, made
                dve.wait_ge(route_full, 2)
                step(dve.tensor_scalar(places, member, -NO_SLOT, NO_SLOT, ALU.mult, ALU.add))
                step(dve.tensor_tensor(places, places, bank[1][:, 0:16].rearrange("p (t e) -> p t e", t=NT), ALU.add))
                step(dve.tensor_copy(slot_of[:, :, 0:8], places))
                step(dve.tensor_copy(gate_of[:, :, 0:8], gates))
                step(dve.memset(slot_of[:, :, JOBS_MAX:JOBS_MAX + 1], NO_SLOT))
                step(dve.memset(gate_of[:, :, JOBS_MAX:JOBS_MAX + 1], 0.0))
                step(dve.tensor_copy(count, bank[1][:, 16:24]))
                step(dve.tensor_scalar(over_e, count, float(P), None, ALU.is_gt))
                step(dve.tensor_copy(incl[:, 0:1], over_e[:, 0:1]))
                for e in range(1, 8):
                    step(dve.tensor_tensor(incl[:, e:e + 1], incl[:, e - 1:e], over_e[:, e:e + 1], ALU.add))
                step(dve.tensor_tensor(before, incl, over_e, ALU.subtract))
                for k in range(3):
                    step(dve.scalar_tensor_tensor(out=sel, in0=before, scalar=float(k), in1=over_e, op0=ALU.is_equal,
                                                  op1=ALU.mult, accum_out=cnt_k[:, k:k + 1]))
                    step(dve.scalar_tensor_tensor(out=junk[:, 0, :], in0=sel, scalar=1.0, in1=slots_iota[:, 0:8],
                                                  op0=ALU.mult, op1=ALU.mult, accum_out=ids[:, k:k + 1]))
                    step(dve.tensor_scalar(none_k[:, k:k + 1], cnt_k[:, k:k + 1], -NO_SLOT, NO_SLOT, ALU.mult, ALU.add))
                    for t in range(NT):
                        step(dve.scalar_tensor_tensor(out=junk[:, t, :], in0=places[:, t, :], scalar=-float(P), in1=sel,
                                                      op0=ALU.add, op1=ALU.mult, accum_out=s_k[:, k, t:t + 1]))
                        step(dve.tensor_tensor(slot_of[:, t, E + k:E + k + 1], s_k[:, k, t:t + 1], none_k[:, k:k + 1], ALU.add))
                        step(dve.scalar_tensor_tensor(out=junk[:, t, :], in0=gates[:, t, :], scalar=1.0, in1=sel,
                                                      op0=ALU.mult, op1=ALU.mult, accum_out=gate_of[:, t, E + k:E + k + 1]))
                step(dve.tensor_copy(ids[:, 3:4], incl[:, 7:8]))
                dve.tensor_copy(route_i[:, :], ids).then_inc(routed, 1)

            dve.wait_ge(setup_free, 5)
            with dve.Fori(0, DEPTH) as layer:
                lo_chunk(layer, CHUNKS[0])
                norm(layer, norm_dve, norm_act, "mix ", x, tok)
                for q in range(4):
                    split_scaled(layer, f"h{q}", stat0, [(2 * q, 2 * q), (2 * q + 1, 2 * q + 1)])
                for c, after in zip(CHUNKS, CHUNKS[1:] + [None]):
                    if after is not None:
                        lo_chunk(layer, after)
                    slot_work(layer, c.name)
                with dve.If(layer == 0):
                    feed_forward(DENSE_BASE, 0, 0)
                    take_layer_constants(1)
                    dve.wait_ge(ffn_acc.sem, ffn_acc.at(UNITS - 1, "half1"))
                with dve.Else():
                    route()
                    dve.memset(wpick_t, 0.0).then_inc(picks_copied.sem, 1)
                    pick_slots(0)
                    gathered(0)
                    dve.wait_ge(routed, 1)
                    n_jobs = dve.value_load(route_i[0:1, 3:4], min_val=0, max_val=3) + E
                    with dve.Fori(0, n_jobs) as j:
                        feed_forward(job_base(j), j * UNITS, 1, j)
                        gathered(j + 1)
                    scattered(n_jobs)
                    dve.wait_ge(scatter_added.sem, scatter_added.at(n_jobs, "t1"))
                    dve.memset(pos_f[:, :], 0.0).then_inc(x_stands, 1)
                dve.nop()
            norm(1, ends_dve, ends_act, "", x, tok)
            dve.wait_ge(final_landed, 16)
            for t, s in ((0, ends_act), (1, ends_dve)):
                dve.wait_ge(s.sem, s.at(1, "scaled"))
                dve.tensor_tensor(tok[:, t, :], tok[:, t, :], final_gain, ALU.mult).then_inc(final_rows, 1)

        @block.tensor
        def _(pe):
            def product(dst, stationary, k, cols, b, kt, n, start, stop):
                x_hi, x_lo = stationary[:, 0, k, cols], stationary[:, 1, k, cols]
                wh, wl = w_hi[:, slot(b), kt, 0:n], w_lo[:, slot(b), kt, 0:n]
                pe.matmul(dst, x_hi, wh, start=start, stop=False)
                pe.matmul(dst, x_hi, wl, start=False, stop=False)
                return pe.matmul(dst, x_lo, wh, start=False, stop=stop)

            def consume(b, stationary, k0, dsts, n, first, last):
                pe.wait_ge(lo_done, number(b) + (1 + RAW_SLOTS))
                for t, dst in enumerate(dsts):
                    for kt in range(4):
                        ins = product(dst[:, 0:n], stationary, k0 + kt, slice(t * P, (t + 1) * P), b, kt, n,
                                      first and kt == 0, last and kt == 3)
                ins.then_inc(block_used, 1)

            def gemm(layer, c, stationary, k0=0):
                i = CHUNKS.index(c)
                if i >= 2:
                    pe.wait_ge(acc_sem(CHUNKS[i - 2]), released_at(layer, CHUNKS[i - 2]))
                for j in range(c.blocks):
                    consume(chunk_block(layer, c, j), stationary, k0 + 4 * j, [acc(c, t) for t in range(NT)], c.n,
                            j == 0, j == c.blocks - 1)

            def opened(layer, name):
                i = SMALL.index(name)
                if i >= 4:
                    pe.wait_ge(bank_sem(SMALL[i - 4]), emptied_at(layer, SMALL[i - 4]))
                return small(name)

            def transposes(layer, name, tiles):
                b = opened(layer, name)
                for i, src in enumerate(tiles):
                    ins = pe.transpose(b[:, i * P:(i + 1) * P], src, ident[:, :])
                ins.then_inc(small_full.sem, 1)

            def rows_t(layer, name, src, q):
                transposes(layer, name, [src[:, t, k * P:(k + 1) * P] for k in (2 * q, 2 * q + 1) for t in range(NT)])

            def scores_of(layer, g):
                t, q0, kt_ = int(g[1]), (5 if g[0] == "a" else 0), (4 if g[0] == "a" else 9)
                nk, banks = P * (t + 1), 2 * (t + 1)
                hn = 8 // banks
                for i in range(banks):
                    b = opened(layer, f"s_{g}_{i}")
                    for j in range(hn):
                        h = i * hn + j
                        rows = slice((h // 4) * 64, (h // 4) * 64 + 64)
                        ins = pe.matmul(b[:, j * nk:(j + 1) * nk], heads_t[rows, q0 + h % 4, t * P:(t + 1) * P],
                                        heads_t[rows, kt_, 0:nk], start=True, stop=True)
                    ins.then_inc(small_full.sem, 1)

            def probs_of(layer, g):
                t = int(g[1])
                pe.wait_ge(soft_act[g].sem, soft_act[g].at(layer, "exp"))
                for i in range(2 * (t + 1)):
                    per = 4 // (t + 1)
                    transposes(layer, f"p_{g}_{i}", [scores[:, i * per + j, k * P:(k + 1) * P]
                                                     for j in range(per) for k in range(t + 1)])

            def outs_of(layer, g):
                t, which = int(g[1]), (0 if g[0] == "a" else 1)
                b = opened(layer, f"o_{g}")
                for i in range(max(0, 2 * (t + 1) - 4), 2 * (t + 1)):
                    pe.wait_ge(bank_sem(f"p_{g}_{i}"), emptied_at(layer, f"p_{g}_{i}"))
                for h in range(8):
                    for k in range(t + 1):
                        ins = pe.matmul(b[:, h * 64:(h + 1) * 64], probs_t[:, h * (t + 1) + k, :],
                                        v_ab[:, k, which, (h // 4) * 64:(h // 4) * 64 + 64], start=(k == 0), stop=(k == t))
                ins.then_inc(small_full.sem, 1)

            def index_logits(layer, t):
                nk = P * (t + 1)
                for i, name in enumerate(("lg1a", "lg1b") if t else ("lg0a", "lg0b")):
                    b = opened(layer, name)
                    rows = slice(i * 64, i * 64 + 64)
                    for j in range(2):
                        ins = pe.matmul(b[:, j * nk:(j + 1) * nk], heads_t[rows, 10 + j, t * P:(t + 1) * P],
                                        heads_t[rows, 12, 0:nk], start=True, stop=True)
                    ins.then_inc(small_full.sem, 1)

            def turned(layer, name, n):
                for t in range(NT):
                    pe.wait_ge(rope_add.sem, rope_add.at(layer, f"{name}{t}"))
                    transposes(layer, f"tr_{name}{t}", [roped[:, t, i * P:(i + 1) * P] for i in range(n)])

            def branch_t(layer, letter, which):
                for t in range(NT):
                    transposes(layer, f"t{letter}{t}", [o_buf[:, which, t, i * P:(i + 1) * P] for i in range(4)])

            def cross_scores(layer, t):
                for i in range(2):
                    b = opened(layer, f"xs{t}{i}")
                    for j in range(2):
                        for d in range(2):
                            ins = pe.matmul(b[:, j * T:(j + 1) * T], qT_x[:, 2 * (2 * i + j) + d, t * P:(t + 1) * P],
                                            kT_x[:, 2 * (2 * i + j) + d, :], start=(d == 0), stop=(d == 1))
                    ins.then_inc(small_full.sem, 1)

            def cross_probs(layer, t):
                for i in range(2):
                    pe.wait_ge(bank_sem(f"xs{t}{i}"), emptied_at(layer, f"xs{t}{i}"))
                for i in range(2):
                    transposes(layer, f"xp{t}{i}", [xs_scores[:, 2 * i + j, k * P:(k + 1) * P]
                                                    for j in range(2) for k in range(2)])

            def cross_outs(layer, t):
                for i in range(2):
                    b = opened(layer, f"xo{t}{i}")
                    pe.wait_ge(bank_sem(f"xp{t}{i}"), emptied_at(layer, f"xp{t}{i}"))
                    for j in range(2):
                        h = 2 * i + j
                        for k in range(2):
                            ins = pe.matmul(b[:, j * T:(j + 1) * T], x_probs_t[:, 2 * h + k, :],
                                            v_tok[:, k, h * T:(h + 1) * T], start=(k == 0), stop=(k == 1))
                    ins.then_inc(small_full.sem, 1)

            def slot_work(layer, name):
                if name == "idx":
                    pe.wait_ge(acc_sem(CH["pu"]), released_at(layer, CH["pu"]))
                    for i in range(2):
                        b = opened(layer, f"pool{i}")
                        for j in range(2):
                            g, at = 2 * i + j, j * T
                            cols = slice(g * P, (g + 1) * P)
                            pe.matmul(b[:, at:at + P], pu_rv[:, 0, cols], pool_m0[:, g, 0:P], start=True, stop=True)
                            pe.matmul(b[:, at + P:at + T], pu_rv[:, 1, cols], pool_m1[:, g, :], start=True, stop=False)
                            ins = pe.matmul(b[:, at + P:at + P + 16], pu_rv[:, 0, cols], pool_m0[:, g, P:144],
                                            start=False, stop=True)
                        ins.then_inc(small_full.sem, 1)
                elif name == "bq":
                    pe.wait_ge(pool_w_landed, (layer + 1) * 16)
                    for i in range(2):
                        b = opened(layer, f"pooly{i}")
                        pe.wait_ge(bank_sem(f"pool{i}"), emptied_at(layer, f"pool{i}"))
                        for j in range(2):
                            ins = pe.matmul(b[:, j * T:(j + 1) * T], pw[:, 2 * i + j, :], pooled_t[:, 2 * i + j, :],
                                            start=True, stop=True)
                        ins.then_inc(small_full.sem, 1)
                    turned(layer, "idx", 3)
                elif name == "kv":
                    turned(layer, "bq", 4)
                    for t in range(NT):
                        pe.wait_ge(bank_sem(f"tr_idx{t}"), emptied_at(layer, f"tr_idx{t}"))
                    index_logits(layer, 0)
                elif name == "aq":
                    turned(layer, "kv", 2)
                    index_logits(layer, 1)
                elif name == "rqk":
                    turned(layer, "aq", 4)
                elif name == "rv":
                    turned(layer, "rqk", 4)
                    for t in range(NT):
                        pe.wait_ge(bank_sem(f"tr_aq{t}"), emptied_at(layer, f"tr_aq{t}"))
                    scores_of(layer, "a0")
                elif name == "rg":
                    for t in range(NT):
                        pe.wait_ge(bank_sem(f"tr_rqk{t}"), emptied_at(layer, f"tr_rqk{t}"))
                    for h in range(4):
                        b = opened(layer, f"st{h}")
                        rows = slice((h % 2) * 64, (h % 2) * 64 + 64)
                        q, k = heads_t[rows, 13 + h // 2, :], heads_t[rows, 15 + h // 2, :]
                        pe.matmul(b[:, 0:T], k[:, 0:P], q[:, 0:T], start=True, stop=True)
                        pe.matmul(b[:, T:T + P], k[:, P:T], q[:, P:T], start=True, stop=True).then_inc(small_full.sem, 1)
                elif name == "gateD0":
                    pe.wait_ge(acc_sem(CH["rv"]), released_at(layer, CH["rv"]))
                    for t in range(NT):
                        b = opened(layer, f"ro{t}")
                        for h in range(4):
                            if t == 0:
                                pe.wait_ge(bank_sem(f"st{h}"), emptied_at(layer, f"st{h}"))
                            cols = slice(h * P, (h + 1) * P)
                            ins = pe.matmul(b[:, cols], decayed[:, h, t * P:(t + 1) * P], pu_rv[:, 0, cols],
                                            start=True, stop=(t == 0))
                            if t:
                                ins = pe.matmul(b[:, cols], decayed[:, h, T:T + P], pu_rv[:, 1, cols],
                                                start=False, stop=True)
                        ins.then_inc(small_full.sem, 1)
                elif name == "upD0":
                    probs_of(layer, "a0")
                elif name == "gateD1":
                    outs_of(layer, "a0")
                elif name == "upD1":
                    pe.wait_ge(bank_sem("ro0"), emptied_at(layer, "ro0"))
                    pe.wait_ge(bank_sem("ro1"), emptied_at(layer, "ro1"))
                    branch_t(layer, "C", 0)
                elif name == "gateC0":
                    scores_of(layer, "a1")
                elif name == "upC0":
                    probs_of(layer, "a1")
                elif name == "gateC1":
                    outs_of(layer, "a1")
                    scores_of(layer, "b0")
                elif name == "upC1":
                    pe.wait_ge(bank_sem("o_a1"), emptied_at(layer, "o_a1"))
                    branch_t(layer, "A", 1)
                    probs_of(layer, "b0")
                elif name == "gateA0":
                    outs_of(layer, "b0")
                    scores_of(layer, "b1")
                elif name == "upA0":
                    probs_of(layer, "b1")
                elif name == "gateA1":
                    outs_of(layer, "b1")
                elif name == "gateB0":
                    pe.wait_ge(bank_sem("o_b1"), emptied_at(layer, "o_b1"))
                    branch_t(layer, "B", 0)
                elif name == "upB1":
                    pe.wait_ge(up_added.sem, up_added.at(layer, "B1"))
                    for q in range(4):
                        rows_t(layer, f"m{q}", merged, q)
                    pe.wait_ge(bank_sem("m3"), emptied_at(layer, "m3"))
                elif name == "out1":
                    pe.wait_ge(mem_split.sem, mem_split.at(layer, "split"))
                elif name == "xkv1":
                    pe.wait_ge(norm_act.sem, norm_act.at(layer, "cross scaled"))
                    pe.wait_ge(norm_dve.sem, norm_dve.at(layer, "cross scaled"))
                    for q in range(4):
                        rows_t(layer, f"c{q}", tok, q)
                    pe.wait_ge(bank_sem("c3"), emptied_at(layer, "c3"))
                elif name == "xq0":
                    pe.wait_ge(acc_sem(CH["xkv1"]), released_at(layer, CH["xkv1"]))
                    for q in range(4):
                        rows_t(layer, f"xk{q}", k_tok, q)
                elif name == "xkv2":
                    pe.wait_ge(acc_sem(CH["xq1"]), released_at(layer, CH["xq1"]))
                    for q in range(4):
                        rows_t(layer, f"xq{q}", q_tok, q)
                    for q in range(4):
                        pe.wait_ge(bank_sem(f"xq{q}"), emptied_at(layer, f"xq{q}"))
                    cross_scores(layer, 0)
                elif name == "xkv3":
                    cross_probs(layer, 0)
                    cross_scores(layer, 1)
                    pe.wait_ge(acc_sem(CH["xkv3"]), released_at(layer, CH["xkv3"]))
                    cross_outs(layer, 0)
                    cross_probs(layer, 1)
                    cross_outs(layer, 1)
                    for i in range(2):
                        pe.wait_ge(bank_sem(f"xo1{i}"), emptied_at(layer, f"xo1{i}"))
                    for q in range(4):
                        rows_t(layer, f"xt{q}", tok, q)
                    pe.wait_ge(bank_sem("xt3"), emptied_at(layer, "xt3"))
                elif name == "xo1":
                    pe.wait_ge(norm_act.sem, norm_act.at(layer, "ffn scaled"))
                    pe.wait_ge(norm_dve.sem, norm_dve.at(layer, "ffn scaled"))
                    for q in range(4):
                        rows_t(layer, f"f{q}", tok, q)
                    pe.wait_ge(bank_sem("f3"), emptied_at(layer, "f3"))

            def stationary_of(name):
                if name.startswith("up"):
                    return stat1, (0 if name[2] in "DA" else 4)
                if name.startswith("xkv") or name.startswith("xo"):
                    return stat1, 0
                return stat0, 0

            def ready(layer, name):
                if name == "upD0":
                    pe.wait_ge(bank_sem("pooly1"), emptied_at(layer, "pooly1"))
                elif name == "upC0":
                    pe.wait_ge(bank_sem("tC1"), emptied_at(layer, "tC1"))
                elif name == "upA0":
                    pe.wait_ge(bank_sem("tA1"), emptied_at(layer, "tA1"))
                elif name == "upB0":
                    pe.wait_ge(bank_sem("tB1"), emptied_at(layer, "tB1"))

            def feed_forward(base, first, kind, job=None):
                tiles = NT if kind == 0 else 1
                s_tr, s_silu, s_hid, s_lo = (s[kind] for s in (ffn_tr, ffn_silu, ffn_hid, ffn_lo))

                def up_half(u, which):
                    if not (isinstance(u, int) and u == 0):
                        pe.wait_ge((s_hid if which else s_silu).sem, (s_hid if which else s_silu).at(first + (u - 1), "hid" if which else "silu"))
                    gu = gu_block(base, u)
                    for i in range(2):
                        consume(plus(gu, 2 * which + i), stat0, 4 * i, [bank[tiles * which + t] for t in range(tiles)],
                                UNIT, i == 0, i == 1)

                def turn_hidden(u):
                    pe.wait_ge(s_hid.sem, s_hid.at(first + u, "hid"))
                    for t in range(tiles):
                        for k in range(4):
                            ins = pe.transpose(bank[(4 if kind == 0 else 2) + t][:, k * P:(k + 1) * P],
                                               hid[:, t, k * P:(k + 1) * P], ident[:, :])
                    ins.then_inc(s_tr.sem, 1)

                def down(u, guard):
                    pe.wait_ge(s_lo.sem, s_lo.at(first + u, "lo"))
                    dn = down_block(base, u)
                    for half in range(2):
                        if kind == 0:
                            if guard:
                                pe.wait_ge(ffn_acc.sem, ffn_acc.at(u - 1, f"half{half}"))
                            dsts = [bank[(6 if half == 0 else 4) + t] for t in range(NT)]
                            consume(plus(dn, half), stat1, 0, dsts, UNIT, True, True)
                        else:
                            consume(plus(dn, half), stat1, 0, [bank[6 + half]], UNIT, False,
                                    isinstance(u, int) and u == UNITS - 1)

                up_half(0, 0)
                up_half(0, 1)
                if kind:
                    scatter(job)
                    open_sums()
                up_half(1, 0)
                if kind:
                    pe.wait_ge(scatter_added.sem, scatter_added.at(job, "t1"))
                turn_hidden(0)
                if kind:
                    turn_picks(job)
                up_half(1, 1)
                down(0, False)
                with pe.Fori(2, UNITS) as u:
                    up_half(u, 0)
                    if kind == 0:
                        pe.wait_ge(ffn_acc.sem, ffn_acc.at(u - 2, "half1"))
                    turn_hidden(u - 1)
                    up_half(u, 1)
                    down(u - 1, True)
                if kind == 0:
                    pe.wait_ge(ffn_acc.sem, ffn_acc.at(UNITS - 2, "half1"))
                turn_hidden(UNITS - 1)
                if kind:
                    gather(job + 1)
                down(UNITS - 1, True)

            def open_sums(closed=False):
                for half in range(2):
                    pe.matmul(bank[6 + half][:, :], zeros[:, :],
                              zeros[:, :].rearrange("p (a n) -> p a n", a=1).broadcast_to([P, 4, P]),
                              start=True, stop=closed)

            def gather(j):
                pe.wait_ge(pick_ready.sem, pick_ready.at(j, "pick"))
                for i, step in enumerate(("low", "high")):
                    for k in range(4):
                        kt = 4 * i + k
                        for t in range(NT):
                            ins = pe.matmul(bank[4 + i][:, k * P:(k + 1) * P], tok[:, t, kt * P:(kt + 1) * P],
                                            pick[:, t, :], start=(t == 0), stop=(t == NT - 1))
                    ins.then_inc(gather_full.sem, 1)

            def turn_picks(j):
                pe.wait_ge(pick_ready.sem, pick_ready.at(j, "weighted"))
                for t in range(NT):
                    ins = pe.transpose(bank[3][:, t * P:(t + 1) * P], wpick[:, t, :], ident[:, :])
                ins.then_inc(picks_full.sem, 1)

            def scatter(j):
                pe.wait_ge(y_copied.sem, y_copied.at(j, "y"))
                pe.wait_ge(picks_copied.sem, picks_copied.at(j, "picks"))
                for t in range(NT):
                    for half in range(2):
                        ins = pe.matmul(bank[(4 if t == 0 else 2) + half][:, :], wpick_t[:, t, :], y_sb[:, half * 512:(half + 1) * 512],
                                        start=True, stop=True)
                    ins.then_inc(scatter_full.sem, 1)

            pe.sem_inc(block_used, SPLIT_SLOTS)
            pe.wait_ge(inputs_landed, 16 * N_SMALL_LOADS)
            pe.wait_ge(consts_ready, 1)
            pe.transpose(bank[0][:, 0:72], gain_rows[0:72, :], ident[0:72, 0:72]).then_inc(setup_full, 1)
            pe.wait_ge(ends_act.sem, ends_act.at(0, "scaled"))
            pe.wait_ge(ends_dve.sem, ends_dve.at(0, "scaled"))
            for q in range(4):
                for i in range(4):
                    ins = pe.transpose(bank[4 + q][:, i * P:(i + 1) * P],
                                       k_tok[:, i % 2, (2 * q + i // 2) * P:(2 * q + i // 2 + 1) * P], ident[:, :])
                ins.then_inc(setup_full, 1)
            pe.wait_ge(setup_free, 5)
            pe.wait_ge(consts_ready, 3)

            with pe.Fori(0, DEPTH) as layer:
                pe.wait_ge(norm_act.sem, norm_act.at(layer, "mix scaled"))
                pe.wait_ge(norm_dve.sem, norm_dve.at(layer, "mix scaled"))
                for q in range(4):
                    rows_t(layer, f"h{q}", tok, q)
                pe.wait_ge(bank_sem("h3"), emptied_at(layer, "h3"))
                for c in CHUNKS:
                    ready(layer, c.name)
                    gemm(layer, c, *stationary_of(c.name))
                    slot_work(layer, c.name)
                with pe.If(layer == 0):
                    feed_forward(DENSE_BASE, 0, 0)
                with pe.Else():
                    for t in range(NT):
                        for k in range(KD):
                            tile = slice(t * P, (t + 1) * P)
                            dst = bank[0][:, 8 * t:8 * t + 8]
                            pe.matmul(dst, stat0[:, 0, k, tile], rw_hi[:, k, :], start=(k == 0), stop=False)
                            pe.matmul(dst, stat0[:, 0, k, tile], rw_lo[:, k, :], start=False, stop=False)
                            ins = pe.matmul(dst, stat0[:, 1, k, tile], rw_hi[:, k, :], start=False, stop=(k == KD - 1))
                    ins.then_inc(route_full, 1)
                    pe.wait_ge(route_dve, ROUTE_MEMBER)
                    member = rt_area[:, 96:112].rearrange("p (t e) -> p t e", t=NT)
                    pe.matmul(bank[1][:, 0:8], triu[:, :], member[:, 0, :], start=True, stop=True)
                    pe.matmul(bank[1][:, 8:16], triu[:, :], member[:, 1, :], start=True, stop=False)
                    pe.matmul(bank[1][:, 8:16], ones[:, :], member[:, 0, :], start=False, stop=True)
                    pe.matmul(bank[1][:, 16:24], ones[:, :], member[:, 0, :], start=True, stop=False)
                    pe.matmul(bank[1][:, 16:24], ones[:, :], member[:, 1, :], start=False, stop=True).then_inc(route_full, 1)
                    open_sums(closed=True)
                    gather(0)
                    pe.wait_ge(routed, 1)
                    n_jobs = pe.value_load(route_i[0:1, 3:4], min_val=0, max_val=3) + E
                    with pe.Fori(0, n_jobs) as j:
                        pe.wait_ge(gather_lo.sem, gather_lo.at(j, "high"))
                        feed_forward(job_base(j), j * UNITS, 1, j)
                    pe.wait_ge(gather_lo.sem, gather_lo.at(n_jobs, "high"))
                    scatter(n_jobs)
                pe.nop()


_INS = ["x", "mem", "positions", "norm_mix", "w_in", "attn_sink", "w_branch", "w_out", "pool_w", "pool_scale",
        "norm_cross", "norm_mem", "w_xq", "w_xkv", "w_xo", "norm_ffn", "dense_w_gu", "dense_w_down", "router_w",
        "moe_w_gu", "moe_w_down", "norm_final"]


def kernel(**inputs):
    import numpy as _np
    import concourse.bacc as _bacc
    from concourse import mybir as _mybir
    from concourse.bass_utils import run_bass_kernel_spmd as _run

    nc = _bacc.Bacc("TRN2", target_bir_lowering=False, num_devices=1)
    arrays, args = {}, []
    for name in _INS:
        a = _np.ascontiguousarray(inputs[name])
        arrays[f"in_{name}"] = a
        args.append(nc.dram_tensor(f"in_{name}", a.shape, _mybir.dt.from_np(a.dtype), kind="ExternalInput").ap())
    args.append(nc.dram_tensor("out_0", inputs["x"].shape, _mybir.dt.float32, kind="ExternalOutput").ap())
    build(nc, *args)
    r = _run(nc, [arrays], core_ids=[0])
    return r.results[0]["out_0"]
```
